# Optimizing a Trainium2 kernel written in Bass

```python
import jax, jax.numpy as jnp
from jax import lax
import numpy as np

D_MODEL = 2048
BATCH = 1
SEQ = 256
DEPTH = 2
DEC_BATCH = 8
DEC_SEQ = 4
PAST_LEN = 2048
PAGE_SIZE = 128

N_META = 16
POOL_WINDOWS = (2, 4, 8, 16)
N_POOL_GROUPS = len(POOL_WINDOWS)
POOL_GROUP = D_MODEL // N_POOL_GROUPS
POOL_STATE = max(POOL_WINDOWS) - 1
HEAD_SIZE = 64
N_HEADS = D_MODEL // HEAD_SIZE
DECAY_LORA = max(32, int(round(1.8 * D_MODEL ** 0.5 / 32)) * 32)
AAA_LORA = max(32, int(round(1.8 * D_MODEL ** 0.5 / 32)) * 32)
MV_LORA = max(32, int(round(1.3 * D_MODEL ** 0.5 / 32)) * 32)
GATE_LORA = max(32, int(round(0.6 * D_MODEL ** 0.8 / 32)) * 32)
D_FF = ((8 * D_MODEL // 3 + 127) // 128) * 128
CONV_WIDTH = 3
N_POOL_LAYERS = (DEPTH + 1) // 2
N_RWKV_LAYERS = DEPTH // 2
NORM_EPS = 1e-6
GN_EPS = 64e-5

kernel_name = "poolformer_rwkv7_convffn_hybrid_step"

def rmsnorm(x, g):
    xf = x.astype(jnp.float32)
    y = xf * lax.rsqrt(jnp.mean(xf * xf, axis=-1, keepdims=True) + NORM_EPS)
    return (y * g.astype(jnp.float32)).astype(x.dtype)

def pool_mixer(h, prefix, start, w_pool, scale):
    B, T, D = h.shape
    ext = jnp.concatenate([prefix.astype(h.dtype), h], axis=1)
    ef = ext.astype(jnp.float32)
    csum = jnp.concatenate([jnp.zeros((B, 1, D), jnp.float32), jnp.cumsum(ef, axis=1)], axis=1)
    end = csum[:, POOL_STATE + 1:]
    pos = start + jnp.arange(T)
    diffs = []
    for g, w in enumerate(POOL_WINDOWS):
        sl = slice(g * POOL_GROUP, (g + 1) * POOL_GROUP)
        begin = csum[:, POOL_STATE + 1 - w: POOL_STATE + 1 - w + T, sl]
        cnt = jnp.minimum(w, pos + 1).astype(jnp.float32)[None, :, None]
        diffs.append((end[..., sl] - begin) / cnt - ef[:, POOL_STATE:, sl])
    d = jnp.stack(diffs, axis=2).astype(h.dtype)
    y = jnp.einsum('btgc,gcd->btgd', d, w_pool).reshape(B, T, D)
    return y * scale, ext[:, -POOL_STATE:]

def wkv7_scan(S0, r, w, k, v, a_in, b_in):
    def step(S, inp):
        r_t, w_t, k_t, v_t, a_t, b_t = inp
        sa = jnp.einsum('bhvk,bhk->bhv', S, a_t)
        S = S * w_t[:, :, None, :] + sa[..., None] * b_t[:, :, None, :] + v_t[..., None] * k_t[:, :, None, :]
        y = jnp.einsum('bhvk,bhk->bhv', S, r_t)
        return S, y
    xs = tuple(jnp.moveaxis(z, 1, 0) for z in (r, w, k, v, a_in, b_in))
    S, ys = lax.scan(step, S0, xs)
    return S, jnp.moveaxis(ys, 0, 1)

def rwkv_mixer(h, shift_prev, S0, v_first, p, j):
    B, T, D = h.shape
    f32 = jnp.float32
    heads = lambda z: z.astype(f32).reshape(B, T, N_HEADS, HEAD_SIZE)
    prev = jnp.concatenate([shift_prev[:, None].astype(h.dtype), h[:, :-1]], axis=1)
    xx = prev - h
    mu = p['rwkv_mu'][j]
    xr, xw, xk, xv, xa, xg = [h + xx * mu[i] for i in range(6)]
    r = xr @ p['rwkv_wr'][j]
    k = xk @ p['rwkv_wk'][j]
    v = xv @ p['rwkv_wv'][j]
    wlog = -jax.nn.softplus(-(p['rwkv_w0'][j] + jnp.tanh(xw @ p['rwkv_w1'][j]) @ p['rwkv_w2'][j]).astype(f32)) - 0.5
    decay = jnp.exp(-jnp.exp(wlog))
    if v_first is None:
        v_first = v
    else:
        jv = j - 1
        v = v + (v_first - v) * jax.nn.sigmoid(p['rwkv_v0'][jv] + (xv @ p['rwkv_v1'][jv]) @ p['rwkv_v2'][jv])
    a = jax.nn.sigmoid(p['rwkv_a0'][j] + (xa @ p['rwkv_a1'][j]) @ p['rwkv_a2'][j])
    g = jax.nn.sigmoid(xg @ p['rwkv_g1'][j]) @ p['rwkv_g2'][j]
    kk = heads(k * p['rwkv_kk'][j])
    kk = kk / jnp.maximum(jnp.sqrt(jnp.sum(kk * kk, axis=-1, keepdims=True)), 1e-12)
    k = k * (1.0 + (a - 1.0) * p['rwkv_ka'][j])
    rh, kh, vh, ah = heads(r), heads(k), heads(v), heads(a)
    S, y = wkv7_scan(S0.astype(f32), rh, heads(decay), kh, vh, -kk, kk * ah)
    mean = jnp.mean(y, axis=-1, keepdims=True)
    var = jnp.mean(jnp.square(y - mean), axis=-1, keepdims=True)
    yn = ((y - mean) * lax.rsqrt(var + GN_EPS)).reshape(B, T, D)
    yn = yn * p['rwkv_lnw'][j].astype(f32) + p['rwkv_lnb'][j].astype(f32)
    bonus = jnp.sum(rh * kh * p['rwkv_rk'][j].astype(f32), axis=-1, keepdims=True) * vh
    out = ((yn + bonus.reshape(B, T, D)).astype(h.dtype) * g) @ p['rwkv_wo'][j]
    return out, h[:, -1], S, v_first

def conv_ffn(h, prefix, w_in, conv_w, conv_b, w_out):
    T = h.shape[1]
    u = h @ w_in
    ext = jnp.concatenate([prefix.astype(u.dtype), u], axis=1)
    c = conv_b + ext[:, 0:T] * conv_w[0]
    for i in range(1, CONV_WIDTH):
        c = c + ext[:, i:i + T] * conv_w[i]
    val, gate = jnp.split(c, 2, axis=-1)
    return (jax.nn.silu(gate) * val) @ w_out, ext[:, -(CONV_WIDTH - 1):]

def trunk(x, start, pool_st, shift_st, wkv_st, conv_st, p):
    new_pool, new_shift, new_wkv, new_conv = [], [], [], []
    v_first = None
    for i in range(DEPTH):
        j = i // 2
        h = rmsnorm(x, p['norm_mix'][i])
        if i % 2 == 0:
            y, st = pool_mixer(h, pool_st[j], start, p['pool_w'][j], p['pool_scale'][j])
            new_pool.append(st)
        else:
            y, sh, S, v_first = rwkv_mixer(h, shift_st[j], wkv_st[j], v_first, p, j)
            new_shift.append(sh)
            new_wkv.append(S)
        x = x + y
        h = rmsnorm(x, p['norm_ffn'][i])
        y, cs = conv_ffn(h, conv_st[i], p['ffn_w_in'][i], p['ffn_conv_w'][i], p['ffn_conv_b'][i], p['ffn_w_out'][i])
        new_conv.append(cs)
        x = x + y
    return (rmsnorm(x, p['norm_out']), jnp.stack(new_pool), jnp.stack(new_shift),
            jnp.stack(new_wkv), jnp.stack(new_conv))

def setup_inputs(seed: int = 0) -> dict:
    key = jax.random.key(seed)
    ks = iter(jax.random.split(key, 48))
    f32 = jnp.float32
    nrm = lambda shape, s: jax.random.normal(next(ks), shape, f32) * s
    D, NP, NR = D_MODEL, N_POOL_LAYERS, N_RWKV_LAYERS
    F2 = 2 * D_FF
    return {
        'x_prompt': nrm((BATCH, SEQ, D), 1.0),
        'x_sample': nrm((DEC_BATCH, DEC_SEQ, D), 1.0),
        'state_pool': nrm((NP, DEC_BATCH, POOL_STATE, D), 1.0),
        'state_rwkv_shift': nrm((NR, DEC_BATCH, D), 1.0),
        'state_rwkv_wkv': nrm((NR, DEC_BATCH, N_HEADS, HEAD_SIZE, HEAD_SIZE), 0.3),
        'state_ffn_conv': nrm((DEPTH, DEC_BATCH, CONV_WIDTH - 1, F2), 1.0),
        'meta_tokens': nrm((N_META, D), 1.0),
        'norm_mix': 1.0 + nrm((DEPTH, D), 0.05),
        'norm_ffn': 1.0 + nrm((DEPTH, D), 0.05),
        'norm_out': 1.0 + nrm((D,), 0.05),
        'pool_w': nrm((NP, N_POOL_GROUPS, POOL_GROUP, POOL_GROUP), POOL_GROUP ** -0.5),
        'pool_scale': 0.5 + nrm((NP, D), 0.05),
        'rwkv_mu': jax.random.uniform(next(ks), (NR, 6, D), f32),
        'rwkv_wr': nrm((NR, D, D), D ** -0.5),
        'rwkv_wk': nrm((NR, D, D), D ** -0.5),
        'rwkv_wv': nrm((NR, D, D), D ** -0.5),
        'rwkv_wo': nrm((NR, D, D), D ** -0.5),
        'rwkv_w0': jax.random.uniform(next(ks), (NR, D), f32, -6.0, 1.0),
        'rwkv_w1': nrm((NR, D, DECAY_LORA), D ** -0.5),
        'rwkv_w2': nrm((NR, DECAY_LORA, D), 0.5 * DECAY_LORA ** -0.5),
        'rwkv_a0': nrm((NR, D), 0.5),
        'rwkv_a1': nrm((NR, D, AAA_LORA), D ** -0.5),
        'rwkv_a2': nrm((NR, AAA_LORA, D), 0.5 * AAA_LORA ** -0.5),
        'rwkv_v0': nrm((NR - 1, D), 0.5),
        'rwkv_v1': nrm((NR - 1, D, MV_LORA), D ** -0.5),
        'rwkv_v2': nrm((NR - 1, MV_LORA, D), 0.5 * MV_LORA ** -0.5),
        'rwkv_g1': nrm((NR, D, GATE_LORA), D ** -0.5),
        'rwkv_g2': nrm((NR, GATE_LORA, D), GATE_LORA ** -0.5),
        'rwkv_kk': 0.85 + nrm((NR, D), 0.05),
        'rwkv_ka': 1.0 + nrm((NR, D), 0.05),
        'rwkv_rk': nrm((NR, N_HEADS, HEAD_SIZE), 0.1),
        'rwkv_lnw': 1.0 + nrm((NR, D), 0.05),
        'rwkv_lnb': nrm((NR, D), 0.01),
        'ffn_w_in': nrm((DEPTH, D, F2), D ** -0.5),
        'ffn_conv_w': nrm((DEPTH, CONV_WIDTH, F2), CONV_WIDTH ** -0.5),
        'ffn_conv_b': nrm((DEPTH, F2), 0.01),
        'ffn_w_out': nrm((DEPTH, D_FF, D), D_FF ** -0.5),
    }

def reference(x_prompt, x_sample, state_pool, state_rwkv_shift, state_rwkv_wkv, state_ffn_conv,
              meta_tokens, norm_mix, norm_ffn, norm_out, pool_w, pool_scale,
              rwkv_mu, rwkv_wr, rwkv_wk, rwkv_wv, rwkv_wo, rwkv_w0, rwkv_w1, rwkv_w2,
              rwkv_a0, rwkv_a1, rwkv_a2, rwkv_v0, rwkv_v1, rwkv_v2, rwkv_g1, rwkv_g2,
              rwkv_kk, rwkv_ka, rwkv_rk, rwkv_lnw, rwkv_lnb,
              ffn_w_in, ffn_conv_w, ffn_conv_b, ffn_w_out):
    p = dict(norm_mix=norm_mix, norm_ffn=norm_ffn, norm_out=norm_out, pool_w=pool_w, pool_scale=pool_scale,
             rwkv_mu=rwkv_mu, rwkv_wr=rwkv_wr, rwkv_wk=rwkv_wk, rwkv_wv=rwkv_wv, rwkv_wo=rwkv_wo,
             rwkv_w0=rwkv_w0, rwkv_w1=rwkv_w1, rwkv_w2=rwkv_w2, rwkv_a0=rwkv_a0, rwkv_a1=rwkv_a1,
             rwkv_a2=rwkv_a2, rwkv_v0=rwkv_v0, rwkv_v1=rwkv_v1, rwkv_v2=rwkv_v2, rwkv_g1=rwkv_g1,
             rwkv_g2=rwkv_g2, rwkv_kk=rwkv_kk, rwkv_ka=rwkv_ka, rwkv_rk=rwkv_rk, rwkv_lnw=rwkv_lnw,
             rwkv_lnb=rwkv_lnb, ffn_w_in=ffn_w_in, ffn_conv_w=ffn_conv_w, ffn_conv_b=ffn_conv_b,
             ffn_w_out=ffn_w_out)
    B, dt = x_prompt.shape[0], x_prompt.dtype
    xp = jnp.concatenate([jnp.broadcast_to(meta_tokens.astype(dt)[None], (B, N_META, D_MODEL)), x_prompt], axis=1)
    zp_pool = jnp.zeros((N_POOL_LAYERS, B, POOL_STATE, D_MODEL), dt)
    zp_shift = jnp.zeros((N_RWKV_LAYERS, B, D_MODEL), dt)
    zp_wkv = jnp.zeros((N_RWKV_LAYERS, B, N_HEADS, HEAD_SIZE, HEAD_SIZE), jnp.float32)
    zp_conv = jnp.zeros((DEPTH, B, CONV_WIDTH - 1, 2 * D_FF), dt)
    yp, pool_p, shift_p, wkv_p, conv_p = trunk(xp, 0, zp_pool, zp_shift, zp_wkv, zp_conv, p)
    y_prompt = yp[:, N_META:]
    y_sample, pool_s, shift_s, wkv_s, conv_s = trunk(x_sample, PAST_LEN, state_pool, state_rwkv_shift,
                                                     state_rwkv_wkv, state_ffn_conv, p)
    return (y_prompt, y_sample, pool_p, pool_s, shift_p, shift_s, wkv_p, wkv_s, conv_p, conv_s)


_drawn_inputs = setup_inputs


def setup_inputs(seed=0):
    import zlib

    import numpy as np

    out = dict(_drawn_inputs(seed))
    spreads = {}
    factors = {'rwkv_lnw': 2.879, 'rwkv_lnb': 8.0, 'ffn_conv_b': 5.466}
    for name, (base, spread) in spreads.items():
        noise = np.random.default_rng([zlib.crc32(name.encode()), seed]).standard_normal(out[name].shape)
        drawn = base * np.exp(spread * noise) if base else spread * noise
        out[name] = __import__('jax').numpy.asarray(drawn.astype(out[name].dtype))
    for name, factor in factors.items():
        out[name] = (out[name] * factor).astype(out[name].dtype)
    return out
```

```python
import numpy as np

import concourse.bass as bass
from concourse import mybir
from contextlib import ExitStack

D = 2048
N_META, SEQ = 16, 256
PROMPT = N_META + SEQ
NSEQ, TSAMPLE = 8, 4
TOK = PROMPT + NSEQ * TSAMPLE
KT = D // 128
D_FF = 5504
FT = D_FF // 128
LAYERS = 2
POOL_STATE = 15
WINDOWS = (2, 4, 8, 16)
HEADS, HS = 32, 64
PAIRS = HEADS // 2
C = 64
CHUNKS = 5
PADTOK = C * CHUNKS
TAIL = 4 * C
TAILP = PROMPT - TAIL
EXT = 2 + PROMPT + NSEQ * (2 + TSAMPLE)
CONVW = EXT - 2
PEXT = POOL_STATE + PROMPT + NSEQ * (POOL_STATE + TSAMPLE)
PS0 = POOL_STATE + PROMPT
NORM_EPS = 1e-6
GN_EPS = 64e-5
LORA = 96
RSTEPS = 12
DECAY_SCALE = -float(np.exp(-0.5))

SEGS = (16, 16, 11)
SEG0 = (0, 16, 32)
PHASES = [("pool", 2, (8, 8, 8, 8))]


def _ffn_phases(layer):
    for s, n in enumerate(SEGS):
        PHASES.append((f"in{layer}{s}", n, (8, 8, 8, 8)))
        PHASES.append((f"out{layer}{s}", 8, (8, n - 8, 8, n - 8)))


_ffn_phases(0)
PHASES += [("lora", 2, (8, 8, 8, 8)), ("k", 8, (8, 8, 8, 8)), ("r", 8, (8, 8, 8, 8)),
           ("v", 8, (8, 8, 8, 8)), ("o", 8, (8, 8, 8, 8))]
_ffn_phases(1)
FIRST, COUNT = {}, {}
_g = 0
for _n, _c, _s in PHASES:
    FIRST[_n], COUNT[_n] = _g, _c
    _g += _c
GROUPS = _g

PCOL = {n: 16 * i for i, n in enumerate(
    ["mix0", "ffn0", "mix1", "ffn1", "out", "scale", "mu0", "mu1", "mu2", "mu3", "mu4", "mu5",
     "w0", "a0", "kk", "ka", "lnw", "lnb", "rk"])}
NPAR = 16 * len(PCOL)

CCOL, _at = {}, 0
for _n, _w in [("ident", 128), ("bones", 128), ("half", 2), ("stk", 192), ("stk_tail", 192),
               ("lt", 128), ("lt_tail", 128), ("lev", 6 * 128), ("seq", 9), ("rcnt", 4 * TOK)]:
    CCOL[_n] = (_at, _w)
    _at += _w
NCON = _at
NRES = CCOL["rcnt"][0]


def constants():
    out = np.zeros((128, NCON), np.float32)

    def put(name, a):
        at, w = CCOL[name]
        out[:, at:at + w] = np.asarray(a, np.float32).reshape(128, w)

    p = np.arange(128)
    head, row = p // 64, p % 64
    put("ident", np.eye(128))
    put("bones", head[:, None] == head[None, :])
    put("half", head[:, None] == np.arange(2)[None, :])
    t = np.arange(64)
    seq = np.where(t < TAILP, 8, np.minimum((t - TAILP) // TSAMPLE, 7))
    dead = t >= TAILP + NSEQ * TSAMPLE
    for tail in (False, True):
        same = (seq[row][:, None] == seq[None, :]) & ~dead[row][:, None] & ~dead[None, :] if tail else np.ones((128, 64), bool)
        strict = same & (row[:, None] < t[None, :])
        upto = same & (row[:, None] <= t[None, :])
        suffix = "_tail" if tail else ""
        put("stk" + suffix, np.concatenate([upto, strict, upto], 1))
        put("lt" + suffix, np.concatenate([strict * (head == 0)[:, None], strict * (head == 1)[:, None]], 1))
    lev = []
    for l in range(6):
        m = 1 << l
        block = (p[:, None] // (2 * m)) == (p[None, :] // (2 * m))
        low = block & (p[:, None] % (2 * m) >= m) & (p[None, :] % (2 * m) < m)
        lev.append((low.T if l == 0 else low) + np.eye(128))
    put("lev", np.concatenate(lev, 1))
    put("seq", (seq[row][:, None] == np.arange(9)[None, :]) & ~dead[row][:, None])
    tok = np.arange(TOK)
    cnt = np.stack([np.where(tok < PROMPT, np.minimum(w, tok + 1), w) for w in WINDOWS])
    put("rcnt", np.tile((np.float32(1) / cnt.astype(np.float32)).reshape(1, -1), (128, 1)))
    return out


def ds(i, n=1):
    return slice(i, i + n) if isinstance(i, int) else bass.ds(i, n)


class Steps:

    def __init__(self, eng, sem):
        self.eng, self.sem, self.base, self.off = eng, sem, 0, 0

    def done(self, ins):
        ins.then_inc(self.sem, 1)
        self.off += 1
        return ins

    def wait(self):
        self.eng.wait_ge(self.sem, self.base + self.off)

    def enter(self, i, per):
        self.start, self.per = self.base + self.off, per
        self.base, self.off = self.start + per * i, 0

    def leave(self, count):
        assert self.off == self.per, (self.off, self.per)
        self.base, self.off = self.start + self.per * count, 0




def build(nc, W_all, L2_all, xT, params, ffnpar, consts, pool_st, shift_st, wkv_st, conv_st,
          yT, pool_out, shift_out, wkv_out, conv_out, x_spill):
    f32, f32r = mybir.dt.float32, mybir.dt.float32r
    ALU, ACT = mybir.AluOpType, mybir.ActivationFunctionType

    top = [(nc.sbuf_base + 63) // 64 * 64]

    def sb(name, shape, dt=f32, at=None):
        ptr = top if at is None else at
        t = nc.alloc_sbuf_tensor_at(name, shape, dt, offset=ptr[0]).ap()
        ptr[0] += (4 * int(np.prod(shape[1:])) + 31) // 32 * 32
        assert ptr[0] <= nc.sbuf_usable_end, (name, ptr[0])
        return t

    RAW = [sb(f"raw{q}", [128, 8 * 128]) for q in range(4)]
    WHI = [sb(f"whi{q}", [128, 8 * 128], f32r) for q in range(4)]
    WLO = [sb(f"wlo{q}", [128, 8 * 128], f32r) for q in range(4)]
    at_hh = list(top)
    HHI = sb("h_hi", [128, KT, TOK], f32r)
    HLO = sb("h_lo", [128, KT, TOK], f32r)
    PAR = sb("par", [128, NPAR])
    CON = sb("con", [128, NRES])
    w0_half, a0_half, ka_half, ka_rest, kk_neg = [
        sb(n, [128, KT]) for n in ("w0_half", "a0_half", "ka_half", "ka_rest", "kk_neg")]
    at_sq = list(top)
    squares, sumsq, meansq, rnorm = [sb(n, [128, TOK]) for n in ("squares", "sumsq", "meansq", "rnorm")]
    ones = sb("ones", [128, 128])
    at_mix = list(top)
    mix = [sb(f"mix{i}", [128, TOK]) for i in range(2)]
    at_x = list(top)
    x = sb("x", [128, KT, TOK])
    at = list(top)
    pext = sb("pext", [128, KT, PEXT], at=at)
    win = [sb(f"win{i}", [128, 4, PEXT], at=at) for i in range(2)]
    rcnt = sb("rcnt", [128, 4, TOK], at=at)
    pdiff = sb("pdiff", [128, 4, TOK], at=at)
    at = list(top)
    AHI = sb("act_hi", [128, 16, TOK], f32r, at=at)
    ALO = sb("act_lo", [128, 16, TOK], f32r, at=at)
    uext = [sb(f"uext{i}", [128, EXT], at=at) for i in range(2)]
    conv = [sb(f"conv{i}", [128, CONVW], at=at) for i in range(2)]
    sgate = sb("sgate", [128, CONVW], at=at)
    act_f = sb("act_f", [128, TOK], at=at)
    prefix = sb("prefix", [128, 2 * FT, 16], at=at)
    ulast = sb("ulast", [128, 2 * FT, 18], at=at)
    fpar = sb("fpar", [128, 2 * FT, 4], at=at)
    at = list(top)
    k_all = sb("k_all", [128, KT, TOK], at=at)
    r_all = sb("r_all", [128, KT, TOK], at=at)
    hidden = sb("hidden", [128, 4, TOK], at=at)
    at_h = list(at)
    h = sb("h", [128, KT, TOK], at=at)
    xx = sb("xx", [128, KT, TOK], at=at)
    shprev = sb("shift_prev", [128, KT, NSEQ], at=at)
    shlast = sb("shift_last", [128, KT, 9], at=at)
    v_all = sb("v_all", [128, KT, TOK], at=at_h)
    AR = [sb(f"ar{i}", [128, 2, PADTOK], at=at_hh) for i in range(2)]
    TK = [[sb(f"tok_{n}{i}", [128, CHUNKS, 128], at=at_hh) for n in "bkv"] for i in range(2)]
    STK = [sb(f"stk{i}", [128, CHUNKS, 3, C], at=at_hh) for i in range(2)]
    XT = [sb(f"xt{i}", [128, CHUNKS, 128], at=at_hh) for i in range(2)]
    PP = [sb(f"pprod{i}", [128, TOK], at=at_hh) for i in range(2)]
    RT, RHS, SS, SP = [sb(n, [128, 128], at=at_hh) for n in ("rt", "rhs", "ss", "sp")]
    assert at_hh[0] <= at_sq[0]
    GG = [sb(f"gg{i}", [128, TOK], at=at_x) for i in range(2)]
    BON = [sb(f"bonus{i}", [128, TOK], at=at_x) for i in range(2)]
    DEC, NKK, PIN, TA, TB, TC, KP, PPT = [
        sb(n, [128, PADTOK], at=at_x) for n in ("decay", "nkk", "pinv", "ta", "tb", "tc", "kp", "ppt")]
    SOUT = sb("sout", [128, 9, C], at=at_x)
    SA = sb("sa", [128, 128], at=at_x)
    assert at_x[0] <= top[0]
    BD = [sb(n, [128, CHUNKS, 2, C], at=at_h) for n in ("bd_b", "bd_k", "bd_v")]
    LT = sb("lt", [128, CHUNKS, 128], at=at_h)
    XM = sb("xm", [128, CHUNKS, 128], at=at_h)
    T1 = sb("t1", [128, CHUNKS, 128], at=at_h)
    S0 = sb("s0bd", [128, NSEQ, 128], at=at_h)
    L2 = [sb(f"l2_{i}", [128, 4 * 128], at=at_h) for i in range(2)]
    SAX, VX = sb("sax", [128, 9, C], at=at_h), sb("vx", [128, 9, C], at=at_mix)
    YY, SQ, SD, ZD = [sb(n, [128, TOK], at=at_sq) for n in ("yy", "ysq", "ysd", "restart")]

    bank = [nc.alloc_psum_tensor(f"bank{i}", [128, 512], f32).ap() for i in range(8)]

    def con(name):
        at_, w = CCOL[name]
        return CON[:, at_:at_ + w]

    def par(name, m):
        return PAR[:, ds(PCOL[name] + m)]

    ident, bones = con("ident"), con("bones")
    half = con("half")
    TRANSPOSE, mm_ = nc.tensor.transpose, nc.tensor.matmul

    def sem(name):
        return nc.alloc_semaphore(name)

    raw_loaded = [sem(f"raw_loaded{q}") for q in range(4)]
    (whi_ready, wlo_ready, unit_used, a_free, b_free, in_loaded, pst_loaded, ffn_loaded, shift_loaded,
     pool_stored, conv0_stored, shift_stored, stored, x_done, sq_done, sums_done, ms_done, root_done,
     mix_ready, hhi_ready, h_ready, h0_ready, pdiff_ready, phi_ready, pooled_ready, pool_evac,
     pool_clear, u_ready, c0_ready, silu_ready, gated, acthi_ready, act_ready, ulast_saved,
     hid_ready, spilled, refilled, s0_loaded, chunk_clear, out_tile, shlast_ready) = [
        sem(n) for n in """whi_ready wlo_ready unit_used a_free b_free in_loaded pst_loaded ffn_loaded
        shift_loaded pool_stored conv0_stored shift_stored stored x_done sq_done sums_done ms_done root_done
        mix_ready hhi_ready h_ready h0_ready pdiff_ready phi_ready pooled_ready pool_evac
        pool_clear u_ready c0_ready silu_ready gated acthi_ready act_ready ulast_saved
        hid_ready spilled refilled s0_loaded chunk_clear out_tile shlast_ready""".split()]
    prefix_set = [sem(f"prefix_set{i}") for i in range(2)]
    conv_ready = [sem(f"conv_ready{i}") for i in range(2)]
    l2_loaded = [sem(f"l2_loaded{i}") for i in range(2)]
    vec_step, act_step, pool_step = sem("vec_step"), sem("act_step"), sem("pool_step")
    RSEMS = """lora_mm gate_mm kksum_mm bonus_mm trans_mm gram_mm gates_ready kp_ready kksq_ready kkroot
        bd_ready bdv_ready ar_ready rkk_ready bonus_ready gg_ready tok_act tok_vec pend_ready xt2_ready x2_mm
        x2_ready t1_mm t1_ready xup_mm xtail_mm xtail_ready z_mm out1_mm rt_ready rhs_mm rhs_ready sa_mm sa_ready
        y_mm s_mm sp_ready s_ready y_ready sax_ready vx_ready fin_mm fin_ready mean_mm centered ycsq_ready
        var_mm var_ready gnroot scaled affine out_ready wkv_stored""".split()
    (lora_mm, gate_mm, kksum_mm, bonus_mm, trans_mm, gram_mm, gates_ready, kp_ready, kksq_ready, kkroot,
     bd_ready, bdv_ready, ar_ready, rkk_ready, bonus_ready, gg_ready, tok_act, tok_vec, pend_ready, xt2_ready, x2_mm,
     x2_ready, t1_mm, t1_ready, xup_mm, xtail_mm, xtail_ready, z_mm, out1_mm, rt_ready, rhs_mm, rhs_ready, sa_mm, sa_ready,
     y_mm, s_mm, sp_ready, s_ready, y_ready, sax_ready, vx_ready, fin_mm, fin_ready, mean_mm, centered, ycsq_ready,
     var_mm, var_ready, gnroot, scaled, affine, out_ready, wkv_stored) = [sem(n) for n in RSEMS]
    xset_ready = [sem(f"xset_ready{z}") for z in range(2)]

    LV = 5
    TAIL_LV = 3
    X_BEFORE = [0, 16, 64, 80, 128]
    OUT_X = {"out00": 16, "out01": 32, "out02": 48, "o": 64, "out10": 80, "out11": 96, "out12": 112}
    H_BEFORE = {"ffn0": 0, "mu1": 16, "mu4": 32, "mu5": 48, "mu2": 64, "mu0": 80, "mu3": 96, "o": 112, "ffn1": 128}
    MADE_BEFORE = {n: min(c, 112) for n, c in H_BEFORE.items() if n != "o"}
    MIXES = {"w": "mu1", "a": "mu4", "g": "mu5", "k": "mu2", "r": "mu0", "v": "mu3"}
    def later(n):
        return not isinstance(n, int) or n > 0

    def pipeline(iteration, loop, steps=None, per=0):
        iteration(-1, 1, inverse=False, chain=False)
        iteration(0, 0, chain=False)
        with loop(0, PAIRS // 2 - 1) as g:
            if steps:
                steps.enter(g, 2 * per)
            iteration(2 * g + 1, 1)
            iteration(2 * g + 2, 0)
        if steps:
            steps.leave(PAIRS // 2 - 1)
        iteration(PAIRS - 1, 1, operands=False)
        iteration(PAIRS, 0, operands=False, inverse=False)

    SIZES = {n: s for n, _, s in PHASES}
    NAMES = [n for n, _, _ in PHASES]
    G = FIRST

    def end(name):
        return 4 * (FIRST[name] + COUNT[name])

    def prompt(t):
        return t[..., 0:PROMPT]

    def samples(t):
        return t[:, PROMPT:TOK].rearrange("p (b e) -> p b e", b=NSEQ)

    def ext_samples(t, n):
        return t[:, n + PROMPT:].rearrange("p (b e) -> p b e", b=NSEQ)

    def flat(bd, c):
        return bd[:, c, :, :].rearrange("p a b -> p (a b)")

    with nc.Block() as block:

        @block.sync
        def _(sp):
            def load_group(G_, name, behind=True):
                sizes = SIZES[name]
                for q in range(4):
                    if behind:
                        sp.wait_ge(wlo_ready, 4 * G_ + (q - 3))
                    sp.dma_start(RAW[q][:, 0:sizes[q] * 128], W_all[4 * G_ + q, :, 0:sizes[q] * 128])\
                        .then_inc(raw_loaded[q], 16)

            def load_rest(name, first=1):
                with sp.Fori(0, COUNT[name] - first) as g:
                    load_group(G[name] + first + g, name)

            def load_mlp(layer):
                sp.dma_start(prefix, conv_st[layer]).then_inc(ffn_loaded, 16)
                sp.dma_start(fpar, ffnpar[layer]).then_inc(ffn_loaded, 16)

            sp.dma_start(x, xT).then_inc(in_loaded, 16)
            sp.dma_start(CON, consts[:, 0:NRES]).then_inc(in_loaded, 16)
            sp.dma_start(PAR, params).then_inc(in_loaded, 16)
            sp.dma_start(rcnt, consts[:, NRES:].rearrange("p (g t) -> p g t", g=4)).then_inc(pst_loaded, 16)
            sp.dma_start(pext[:, :, POOL_STATE + PROMPT:], pool_st).then_inc(pst_loaded, 16)
            load_group(0, "pool", False)
            load_group(1, "pool")

            def mlp_loads(layer):
                first = f"in{layer}0"
                load_group(G[first], first)
                if layer == 0:
                    sp.wait_ge(pooled_ready, 4)
                    sp.dma_start(pool_out, pext[:, :, PROMPT:]).then_inc(pool_stored, 16)
                    sp.wait_ge(pool_stored, 16)
                else:
                    sp.wait_ge(x_done, X_BEFORE[3])
                    sp.wait_ge(wkv_stored, 16 * PAIRS)
                load_mlp(layer)
                load_rest(first)
                for s in range(3):
                    if s:
                        load_rest(f"in{layer}{s}", 0)
                    load_rest(f"out{layer}{s}", 0)

            mlp_loads(0)
            load_group(G["lora"], "lora")
            sp.wait_ge(ulast_saved, 2 * FT + 1)
            sp.dma_start(conv_out[0], ulast).then_inc(conv0_stored, 16)
            sp.wait_ge(conv0_stored, 16)
            sp.dma_start(shprev, shift_st).then_inc(shift_loaded, 16)
            load_rest("lora")
            load_rest("k", 0)
            load_rest("r", 0)
            load_rest("v", 0)
            load_group(G["o"], "o")
            sp.wait_ge(shlast_ready, 1)
            sp.dma_start(shift_out, shlast).then_inc(shift_stored, 16)
            sp.dma_start(x_spill, x).then_inc(spilled, 16)
            sp.wait_ge(chunk_clear, 1)
            for i in range(2):
                sp.dma_start(L2[i], L2_all[i]).then_inc(l2_loaded[i], 16)
            sp.dma_start(S0, wkv_st[0].rearrange("p (b n) -> p b n", b=NSEQ)).then_inc(s0_loaded, 16)

            def pair_io(p, i, weights=True, states=True):
                if weights:
                    sp.wait_ge(gg_ready, p)
                    sp.dma_start(L2[1 - i], L2_all[p + 1]).then_inc(l2_loaded[1 - i], 16)
                sp.wait_ge(fin_ready, p)
                sp.dma_start(wkv_out[p - 1].rearrange("p (b n) -> p b n", b=9), SOUT).then_inc(wkv_stored, 16)
                sp.wait_ge(wkv_stored, 16 * p)
                if states:
                    sp.dma_start(S0, wkv_st[p].rearrange("p (b n) -> p b n", b=NSEQ)).then_inc(s0_loaded, 16)

            with sp.Fori(0, PAIRS // 2 - 1) as g:
                pair_io(2 * g + 1, 1)
                pair_io(2 * g + 2, 0)
            pair_io(PAIRS - 1, 1, weights=False)
            pair_io(PAIRS, 0, weights=False, states=False)
            sp.wait_ge(out_ready, PAIRS)
            sp.dma_start(x, x_spill).then_inc(refilled, 16)
            load_rest("o")
            mlp_loads(1)
            sp.wait_ge(ulast_saved, 4 * FT + 1)
            sp.dma_start(conv_out[1], ulast).then_inc(stored, 16)
            with sp.Fori(0, KT) as k:
                sp.wait_ge(out_tile, k + 1)
                sp.dma_start(yT[:, k, :], x[:, k, :]).then_inc(stored, 16)
            sp.wait_ge(stored, 16 * (KT + 1))
            sp.wait_ge(shift_stored, 16)

        @block.tensor
        def _(pe):
            def three(acc, wh, wl, xh, xl, first, last):
                mm_(acc, wh, xh, start=first, stop=False)
                mm_(acc, wh, xl, start=False, stop=False)
                return mm_(acc, wl, xh, start=False, stop=last)

            def accumulate(G_, ab, name, hi, lo, free=True, rows=None):
                sizes = SIZES[name][2 * ab:2 * ab + 2]
                for i in range(2):
                    q = 2 * ab + i
                    pe.wait_ge(wlo_ready, 4 * G_ + (q + 1))
                    if i == 0 and free:
                        pe.wait_ge((a_free, b_free)[ab], G_ - 2)
                    for j in range(sizes[i]):
                        k = 8 * i + j
                        if rows is not None:
                            pe.wait_ge(rows[0], rows[1] + k + 1)
                        w = slice(128 * j, 128 * j + 128)
                        mm = three(bank[ab][:, 0:TOK], WHI[q][:, w], WLO[q][:, w], hi[:, k, :], lo[:, k, :],
                                   k == 0, k == sum(sizes) - 1)
                    mm.then_inc(unit_used, 1)

            def run(name, hi, lo, rows=None, start=0):
                if rows is not None:
                    accumulate(G[name], 0, name, hi, lo, G[name] > 2, rows)
                    accumulate(G[name], 1, name, hi, lo, G[name] > 2)
                    start = 1
                with pe.Fori(0, COUNT[name] - start) as g:
                    for ab in range(2):
                        accumulate(G[name] + start + g, ab, name, hi, lo)

            def norm_sum(i):
                pe.wait_ge(sq_done, KT * (i + 1))
                mm_(bank[7][:, 0:TOK], ones, sumsq, start=True, stop=True).then_inc(sums_done, 1)

            pe.wait_ge(in_loaded, 48)
            pe.wait_ge(pool_clear, 2)
            norm_sum(0)
            for g in range(2):
                for q in range(4):
                    grp = 2 * g + q // 2
                    pe.wait_ge(wlo_ready, 4 * g + q + 1)
                    pe.wait_ge(pooled_ready, grp + 1)
                    if g:
                        pe.wait_ge(pool_evac, 2 * q + 2)
                    for i in range(2):
                        for c in range(4):
                            w = slice(128 * (4 * i + c), 128 * (4 * i + c) + 128)
                            k = 4 * grp + c
                            if g == 0 and q == 3 and i == 1 and c == 0:
                                pe.wait_ge(ms_done, 1)
                            mm = three(bank[2 * q + i][:, 0:TOK], WHI[q][:, w], WLO[q][:, w],
                                       HHI[:, k, :], HLO[:, k, :], c == 0, c == 3)
                    mm.then_inc(unit_used, 1)
            pe.wait_ge(pool_evac, 16)

            def mlp(layer):
                norm_sum(1 + 2 * layer)
                for s in range(3):
                    run(f"in{layer}{s}", HHI, HLO, (h_ready, H_BEFORE[f"ffn{layer}"]) if s == 0 else None)
                    run(f"out{layer}{s}", AHI, ALO, (act_ready, FT * layer + SEG0[s]))

            mlp(0)
            norm_sum(2)
            for i, m in enumerate("wag"):
                accumulate(G["lora"] + i // 2, i % 2, "lora", HHI, HLO, rows=(h_ready, H_BEFORE[MIXES[m]]))
            accumulate(G["lora"] + 1, 1, "lora", HHI, HLO)
            run("k", HHI, HLO, (h_ready, H_BEFORE["mu2"]))
            run("r", HHI, HLO, (h_ready, H_BEFORE["mu0"]))

            def iteration(t, par, operands=True, inverse=True, chain=True):
                n, m, j = t + 1, 1 - par, t - 1
                cols = lambda c: slice(128 * (c % 4), 128 * (c % 4) + 128)

                def t1_products(l, z):
                    cs = [2 * z, 2 * z + 1]
                    if l:
                        pe.wait_ge(xset_ready[z], LV * t + l)
                    else:
                        pe.wait_ge(x2_ready, t + 1)
                    if z and l < TAIL_LV:
                        cs.append(CHUNKS - 1)
                        if l:
                            pe.wait_ge(xtail_ready, TAIL_LV * t + l)
                    for i, c in enumerate(cs):
                        mm = mm_(bank[2 + z][:, cols(i)], LT[:, c, :], XM[:, c, :], start=True, stop=True)
                    mm.then_inc(t1_mm, 1)

                def update_products(l, z):
                    cs = [2 * z, 2 * z + 1] if z < 2 else [CHUNKS - 1]
                    pe.wait_ge(t1_ready, 2 * LV * t + 2 * l + min(z, 1) + 1)
                    for i, c in enumerate(cs):
                        if l < LV - 1:
                            mm_(bank[4 + z][:, cols(i)], XT[par][:, c, :], T1[:, c, :], start=True, stop=True)
                        mm = mm_(bank[4 + z][:, cols(2 + i)], T1[:, c, :], XT[par][:, c, :], start=True, stop=True)
                    mm.then_inc(xtail_mm if z == 2 else xup_mm, 1)

                def rows_product(c):
                    o1 = bank[0][:, 0:128]
                    o1v = o1.rearrange("p (a t) -> p a t", a=2)
                    if c:
                        pe.wait_ge(y_ready, CHUNKS * j + c)
                    elif inverse:
                        pe.wait_ge(x2_ready, t + 1)
                    mm = mm_(o1, TK[m][2][:, c, :], STK[m][:, c, 1:3, :], start=True, stop=True)
                    if c:
                        pe.wait_ge(s_ready, 4 * j + c)
                    if 0 < c < CHUNKS - 1:
                        mm = mm_(o1, SS, AR[m][:, :, C * c:C * c + C], start=False, stop=True, skip_group_check=True)
                    if c == CHUNKS - 1:
                        pe.wait_ge(s0_loaded, 16 * j + 16)
                        mm_(o1v[:, :, 0:TAILP], SS, AR[m][:, :, TAIL:PROMPT], start=False, stop=True, skip_group_check=True)
                        for b in range(NSEQ):
                            a, z = TAILP + TSAMPLE * b, TAILP + TSAMPLE * (b + 1)
                            mm = mm_(o1v[:, :, a:z], S0[:, b, :], AR[m][:, :, TAIL + a:TAIL + z],
                                     start=False, stop=True, skip_group_check=True)
                    mm.then_inc(out1_mm, 1)

                def rhs_transpose(c):
                    pe.wait_ge(rt_ready, CHUNKS * j + c + 1)
                    TRANSPOSE(bank[1][:, 0:128], RT, ident).then_inc(rhs_mm, 1)

                def sa_product(c):
                    pe.wait_ge(rhs_ready, CHUNKS * j + c + 1)
                    mm_(bank[1][:, 128:256], XT[m][:, c, :], RHS, start=True, stop=True).then_inc(sa_mm, 1)

                def state_products(c):
                    pe.wait_ge(sa_ready, CHUNKS * j + c + 1)
                    if c < CHUNKS - 1:
                        mm_(bank[1][:, 256:384], TK[m][0][:, c, :], SA, start=True, stop=False)
                        mm_(bank[1][:, 256:384], TK[m][1][:, c, :], TK[m][2][:, c, :], start=False, stop=True).then_inc(s_mm, 1)
                    mm_(bank[0][:, C:2 * C], SA, STK[m][:, c, 0, :], start=False, stop=True, skip_group_check=True)\
                        .then_inc(y_mm, 1)

                if operands:
                    pe.wait_ge(l2_loaded[m], (8 * n + 16) if m == 0 else (8 * n + 8))
                for s_ in range(LV):
                    if chain:
                        rows_product(s_)
                    if inverse:
                        t1_products(s_, 0)
                        t1_products(s_, 1)
                    if operands and s_ == 0:
                        if later(n):
                            pe.wait_ge(gg_ready, n)
                        pe.wait_ge(kksq_ready, n + 1)
                        mm_(bank[7][:, 0:TOK], bones, TB[:, 0:TOK], start=True, stop=True).then_inc(kksum_mm, 1)
                    if operands and s_ == 1:
                        pe.wait_ge(kkroot, n + 1)
                        mm_(bank[7][:, 0:TOK], L2[m][:, 0:128], hidden[:, 0, :], start=True, stop=True).then_inc(z_mm, 1)
                    if operands and s_ == 2:
                        pe.wait_ge(gates_ready, n + 1)
                        mm_(bank[7][:, 0:TOK], L2[m][:, 128:256], hidden[:, 1, :], start=True, stop=True).then_inc(lora_mm, 1)
                    if chain:
                        rhs_transpose(s_)
                    if inverse:
                        update_products(s_, 0)
                    if chain:
                        sa_product(s_)
                    if inverse:
                        update_products(s_, 1)
                        if s_ < TAIL_LV:
                            update_products(s_, 2)
                    if chain:
                        state_products(s_)
                if chain:
                    pe.wait_ge(y_ready, CHUNKS * j + CHUNKS)
                    pe.wait_ge(sax_ready, j + 1)
                    pe.wait_ge(vx_ready, j + 1)
                    for lo, hi, dst in ((0, 8, bank[1]), (8, 9, bank[0])):
                        mm_(dst[:, 0:C * (hi - lo)], TK[m][0][:, CHUNKS - 1, :], SAX[:, lo:hi, :], start=True, stop=False)
                        mm = mm_(dst[:, 0:C * (hi - lo)], TK[m][1][:, CHUNKS - 1, :], VX[:, lo:hi, :], start=False, stop=True)
                    mm.then_inc(fin_mm, 1)
                if operands:
                    pe.wait_ge(bd_ready, n + 1)
                    pe.wait_ge(bdv_ready, n + 1)
                    if inverse:
                        pe.wait_ge(xset_ready[0], LV * t + LV)
                        pe.wait_ge(xset_ready[1], LV * t + LV)
                        pe.wait_ge(xtail_ready, TAIL_LV * t + TAIL_LV)
                    for i in range(3):
                        for c in range(CHUNKS):
                            dst = bank[2 + i][:, cols(c)] if c < 4 else bank[5][:, 128 * i:128 * i + 128]
                            mm = TRANSPOSE(dst, flat(BD[i], c), ident)
                    mm.then_inc(trans_mm, 1)
                    pe.wait_ge(rkk_ready, n + 1)
                    mm_(bank[6][:, 0:TOK], bones, TB[:, 0:TOK], start=True, stop=True).then_inc(bonus_mm, 1)
                if chain:
                    mm_(bank[7][:, 0:TOK], bones, YY, start=True, stop=True).then_inc(mean_mm, 1)
                if operands:
                    pe.wait_ge(tok_act, n + 1)
                    pe.wait_ge(tok_vec, n + 1)
                    pe.wait_ge(ar_ready, n + 1)
                    for c in range(CHUNKS):
                        for i in range(2):
                            o = 256 * (c % 2) + 128 * i
                            mm = mm_(bank[2 + c // 2][:, o:o + 128], flat(BD[i], c), AR[m][:, :, C * c:C * c + C],
                                     start=True, stop=True)
                    mm.then_inc(gram_mm, 1)
                if chain:
                    pe.wait_ge(ycsq_ready, j + 1)
                    mm_(bank[7][:, 0:TOK], bones, SQ, start=True, stop=True).then_inc(var_mm, 1)
                    pe.wait_ge(fin_ready, j + 1)
                    pe.wait_ge(var_ready, j + 1)
                if operands:
                    mm_(bank[7][:, 0:TOK], L2[m][:, 256:384], hidden[:, 2, :], start=True, stop=False)
                    mm_(bank[7][:, 0:TOK], L2[m][:, 384:512], hidden[:, 3, :], start=False, stop=True).then_inc(gate_mm, 1)
                    pe.wait_ge(xt2_ready, n + 1)
                    for c in range(CHUNKS):
                        mm = TRANSPOSE(bank[5 if c < 4 else 0][:, cols(c)], XT[m][:, c, :], ident)
                    mm.then_inc(x2_mm, 1)

            run("v", HHI, HLO, (h_ready, H_BEFORE["mu3"]))
            pe.wait_ge(hid_ready, 4)
            pe.wait_ge(a_free, G["o"] - 2)
            pe.wait_ge(b_free, G["o"] - 2)
            pipeline(iteration, pe.Fori)
            run("o", HHI, HLO, (h_ready, H_BEFORE["o"]))
            mlp(1)
            norm_sum(4)

        @block.scalar
        def _(act):
            steps = Steps(act, act_step)
            activation = nc.scalar.activation

            def split(G_, name, q, behind=True):
                n = SIZES[name][q] * 128
                act.wait_ge(raw_loaded[q], 16 * G_ + 16)
                if behind:
                    act.wait_ge(unit_used, 4 * G_ + (q - 3))
                activation(WHI[q][:, 0:n], RAW[q][:, 0:n], ACT.Copy).then_inc(whi_ready, 1)

            def norm_root(i):
                act.wait_ge(ms_done, i + 1)
                activation(rnorm, meansq, ACT.Sqrt).then_inc(root_done, 1)

            def split_rows(key, src, free):
                n0 = MADE_BEFORE.get(key)
                if n0 is None:
                    act.wait_ge(out_ready, PAIRS)
                with act.Fori(0, KT // 2) as k:
                    for i in range(2):
                        if n0 is not None:
                            act.wait_ge(mix_ready, n0 + 2 * k + (i + 1))
                        act.wait_ge(unit_used, free)
                        activation(HHI[:, 2 * k + i, :], src(2 * k + i, i), ACT.Copy).then_inc(hhi_ready, 1)

            mixed = lambda k, i: mix[i]

            def up_rows(G_, i, n):
                act.wait_ge(unit_used, 4 * G_ + 2 * i + 2)
                act.wait_ge(conv_ready[i], n + 1)
                act.wait_ge(ulast_saved, 2 * n + 1)
                activation(uext[i][:, 2:2 + PROMPT], prompt(bank[i]), ACT.Copy)
                activation(ext_samples(uext[i], 2)[:, :, 2:], samples(bank[i]), ACT.Copy).then_inc(u_ready, 1)
                act.wait_ge(u_ready, 2 * n + i + 1)
                act.sem_inc((a_free, b_free)[i], 1)
                act.wait_ge(gated, n + 1)
                act.wait_ge(prefix_set[i], n + 1)

            def up(G_, i, n, j):
                col = FT * i + j
                up_rows(G_, i, n)
                activation(conv[i], uext[i][:, 0:CONVW], ACT.Identity, bias=fpar[:, ds(col), 3], scale=fpar[:, ds(col), 0])\
                    .then_inc(c0_ready, 1)
                if i == 1:
                    act.wait_ge(conv_ready[1], n + 2)
                    activation(sgate, conv[1], ACT.Silu).then_inc(silu_ready, 1)
                    act.wait_ge(gated, n + 2)
                    activation(AHI[:, j_local[0], :], act_f, ACT.Copy).then_inc(acthi_ready, 1)

            j_local = [0]

            def evac(name, G_, i, g):
                if name.startswith("in"):
                    layer, s = int(name[2]), int(name[3])
                    j_local[0] = g
                    up(G_, i, FT * layer + SEG0[s] + g, SEG0[s] + g)
                elif name in "krv":
                    act.wait_ge(unit_used, 4 * G_ + 2 * i + 2)
                    dst = {"k": k_all, "r": r_all, "v": v_all}[name]
                    activation(dst[:, 2 * g + i, :], bank[i][:, 0:TOK], ACT.Copy).then_inc((a_free, b_free)[i], 1)
                elif name == "lora":
                    act.wait_ge(unit_used, 4 * G_ + 2 * i + 2)
                    n = 2 * g + i
                    if n == 0:
                        activation(hidden[:, 0, :], bank[i][:, 0:TOK], ACT.Tanh).then_inc(a_free, 1)
                    elif n == 1:
                        activation(hidden[:, 1, :], bank[i][:, 0:TOK], ACT.Copy).then_inc(b_free, 1)
                    else:
                        activation(hidden[:, n, :], bank[i][:, 0:TOK], ACT.Tanh, scale=0.5).then_inc((a_free, b_free)[i], 1)

            def iteration(t, par_, operands=True, inverse=True, chain=True):
                n, m, j = t + 1, 1 - par_, t - 1
                if operands:
                    if later(n):
                        act.wait_ge(bonus_mm, n)
                    activation(TB[:, 0:TOK], k_all[:, n, :], ACT.Square, scale=par("kk", n)).then_inc(kksq_ready, 1)
                for s_ in range(LV):
                    c = CHUNKS * j + s_

                    def x_evac(b, cs, ready):
                        k = len(cs)
                        dst = lambda X: X[:, cs[0]:cs[0] + k, :]
                        src = lambda o: bank[b][:, o:o + 128 * k].rearrange("p (c n) -> p c n", c=k)
                        if s_ < LV - 1:
                            activation(dst(XM), src(0), ACT.Copy)
                        activation(dst(XT[par_]), src(256), ACT.Copy).then_inc(ready, 1)

                    if chain:
                        if 0 < s_ < CHUNKS - 1:
                            act.wait_ge(s_ready, 4 * j + s_)
                            activation(SP, SS, ACT.Copy, scale=PP[m][:, C * s_ + C - 1:C * s_ + C]).then_inc(sp_ready, 1)
                        act.wait_ge(rhs_mm, c + 1)
                        activation(RHS, bank[1][:, 0:128], ACT.Copy).then_inc(rhs_ready, 1)
                    if inverse:
                        act.wait_ge(xup_mm, 2 * LV * t + 2 * s_ + 1)
                        x_evac(4, (0, 1), xset_ready[0])
                    if chain:
                        act.wait_ge(sa_mm, c + 1)
                        activation(SA, bank[1][:, 128:256], ACT.Copy).then_inc(sa_ready, 1)
                    if inverse and s_ < TAIL_LV:
                        act.wait_ge(xtail_mm, TAIL_LV * t + s_ + 1)
                        x_evac(6, (CHUNKS - 1,), xtail_ready)
                    if chain:
                        act.wait_ge(y_mm, c + 1)
                        w = min(C, TOK - C * s_)
                        activation(YY[:, C * s_:C * s_ + w], bank[0][:, C:C + w], ACT.Copy).then_inc(y_ready, 1)
                    if operands and s_ == 0:
                        act.wait_ge(kksum_mm, n + 1)
                        activation(TC[:, 0:TOK], bank[7][:, 0:TOK], ACT.Sqrt).then_inc(kkroot, 1)
                    if operands and s_ == 1:
                        act.wait_ge(z_mm, n + 1)
                        steps.done(activation(DEC[:, 0:TOK], bank[7][:, 0:TOK], ACT.Tanh, bias=w0_half[:, ds(n)], scale=0.5))
                        steps.wait()
                        activation(DEC[:, 0:TOK], DEC[:, 0:TOK], ACT.Exp, scale=0.5 * DECAY_SCALE, bias=decay_bias)\
                            .then_inc(gates_ready, 1)
                    if operands and s_ == 2:
                        act.wait_ge(lora_mm, n + 1)
                        steps.done(activation(TA[:, 0:TOK], bank[7][:, 0:TOK], ACT.Tanh, bias=a0_half[:, ds(n)], scale=0.5))
                        steps.wait()
                        activation(KP[:, 0:TOK], TA[:, 0:TOK], ACT.Identity, scale=ka_half[:, ds(n)], bias=ka_rest[:, ds(n)])\
                            .then_inc(kp_ready, 1)
                if operands:
                    act.wait_ge(trans_mm, n + 1)
                    activation(TK[m][0][:, 0:4, :], bank[2].rearrange("p (c n) -> p c n", c=4), ACT.Copy)
                    activation(TK[m][1][:, 0:4, :], bank[3].rearrange("p (c n) -> p c n", c=4), ACT.Copy).then_inc(tok_act, 1)
                if chain:
                    act.wait_ge(fin_ready, j + 1)
                if operands:
                    act.wait_ge(ar_ready, n + 1)
                    activation(PP[m], PPT[:, 0:TOK], ACT.Copy).then_inc(pend_ready, 1)
                if chain:
                    act.wait_ge(centered, j + 1)
                    activation(SQ, YY, ACT.Square).then_inc(ycsq_ready, 1)
                    act.wait_ge(var_ready, j + 1)
                    activation(SD, SD, ACT.Sqrt).then_inc(gnroot, 1)
                if operands:
                    act.wait_ge(x2_mm, n + 1)
                    activation(XM[:, 0:4, :], bank[5].rearrange("p (c n) -> p c n", c=4), ACT.Copy)
                    activation(XM[:, 4, :], bank[0][:, 0:128], ACT.Copy).then_inc(x2_ready, 1)
                if chain:
                    act.wait_ge(scaled, j + 1)
                    activation(YY, YY, ACT.Identity, scale=par("lnw", j), bias=par("lnb", j)).then_inc(affine, 1)
                    act.wait_ge(out_ready, j + 1)
                if operands:
                    act.wait_ge(gate_mm, n + 1)
                    activation(GG[m], bank[7][:, 0:TOK], ACT.Copy).then_inc(gg_ready, 1)

            decay_bias = 0.5 * DECAY_SCALE
            act.wait_ge(in_loaded, 48)
            for q in range(4):
                split(0, "pool", q, False)
            norm_root(0)
            for grp in range(4):
                act.wait_ge(pdiff_ready, grp + 1)
                activation(HHI[:, 4 * grp:4 * grp + 4, :], pdiff, ACT.Copy).then_inc(phi_ready, 1)
            for q in range(4):
                split(1, "pool", q)

            prev = None

            def transition(name):
                if name == "in00":
                    norm_root(1)
                    act.wait_ge(pool_evac, 16)
                    split_rows("ffn0", mixed, end("pool"))
                elif name == "in10":
                    norm_root(3)
                    split_rows("ffn1", mixed, end("o"))
                elif name in "krv":
                    split_rows(MIXES[name], mixed, {"k": end("lora"), "r": end("k"), "v": end("r")}[name])
                elif name == "o":
                    act.wait_ge(chunk_clear, 1)
                    pipeline(iteration, act.Fori, steps, 2)
                    split_rows("o", lambda k, i: r_all[:, k, :], end("v"))

            for name in NAMES[1:]:
                g0, n = G[name], COUNT[name]
                steady = 1
                for q in range(4):
                    split(g0, name, q)
                    if prev and q % 2:
                        evac(prev, g0 - 1, q // 2, COUNT[prev] - 1)
                if name == "lora":
                    norm_root(2)
                    split_rows("mu1", mixed, end("out02"))
                    split_rows("mu4", mixed, 4 * g0 + 2)
                    evac("lora", g0, 0, 0)
                    for q in range(4):
                        split(g0 + 1, name, q)
                    evac("lora", g0, 1, 0)
                    split_rows("mu5", mixed, 4 * g0 + 4)
                else:
                    transition(name)
                    if n > 1:
                        with act.Fori(0, n - 1) as g:
                            for q in range(4):
                                split(g0 + 1 + g, name, q)
                                if q % 2:
                                    evac(name, g0 + g, q // 2, g)
                prev = name
            norm_root(4)

        @block.vector
        def _(vec):
            steps = Steps(vec, vec_step)
            tt, ts, stt = nc.vector.tensor_tensor, nc.vector.tensor_scalar, nc.vector.scalar_tensor_tensor

            def link(ins):
                steps.done(ins)
                steps.wait()

            def split(G_, name, q):
                n = SIZES[name][q] * 128
                vec.wait_ge(whi_ready, 4 * G_ + q + 1)
                tt(WLO[q][:, 0:n], RAW[q][:, 0:n], WHI[q][:, 0:n].bitcast(f32), ALU.subtract).then_inc(wlo_ready, 1)

            def norm_scale(i):
                vec.wait_ge(sums_done, i + 1)
                ts(meansq, bank[7][:, 0:TOK], 1.0 / D, NORM_EPS, ALU.mult, ALU.add).then_inc(ms_done, 1)
                vec.wait_ge(root_done, i + 1)
                link(nc.vector.reciprocal(rnorm, rnorm))

            def rest_rows(key, make, src):
                n0 = H_BEFORE[key]
                with vec.Fori(0, KT // 2) as k:
                    if make is not None:
                        for i in range(2):
                            make(2 * k + i, i).then_inc(mix_ready, 1)
                    for i in range(2):
                        vec.wait_ge(hhi_ready, n0 + 2 * k + (i + 1))
                        tt(HLO[:, 2 * k + i, :], src(2 * k + i, i), HHI[:, 2 * k + i, :].bitcast(f32), ALU.subtract)\
                            .then_inc(h_ready, 1)
                    vec.wait_ge(h_ready, n0 + 2 * k + 2)

            mixed = lambda k, i: mix[i]

            def mix_rows(m):
                mu = MIXES[m]
                rest_rows(mu, lambda k, i: stt(mix[i], xx[:, k, :], par(mu, k), h[:, k, :], ALU.mult, ALU.add), mixed)

            def evac(name, G_, i, g):
                if name.startswith("in"):
                    layer, s = int(name[2]), int(name[3])
                    n, j = FT * layer + SEG0[s] + g, SEG0[s] + g
                    col = FT * i + j
                    vec.wait_ge(c0_ready, 2 * n + i + 1)
                    for tap in (1, 2):
                        ins = stt(conv[i], uext[i][:, tap:tap + CONVW], fpar[:, ds(col), tap], conv[i], ALU.mult, ALU.add)
                        if tap == 1:
                            link(ins)
                    ins.then_inc(conv_ready[i], 1)
                    if i == 1:
                        vec.wait_ge(silu_ready, n + 1)
                        vec.wait_ge(conv_ready[0], n + 2)
                        tt(act_f[:, 0:PROMPT], conv[0][:, 0:PROMPT], sgate[:, 0:PROMPT], ALU.mult)
                        tt(samples(act_f), ext_tail(conv[0]), ext_tail(sgate), ALU.mult).then_inc(gated, 1)
                        vec.wait_ge(acthi_ready, n + 1)
                        tt(ALO[:, g, :], act_f, AHI[:, g, :].bitcast(f32), ALU.subtract).then_inc(act_ready, 1)
                elif name.startswith("out") or name == "o":
                    vec.wait_ge(unit_used, 4 * G_ + 2 * i + 2)
                    m = 2 * g + i
                    tt(x[:, m, :], bank[i][:, 0:TOK], x[:, m, :], ALU.add).then_inc(x_done, 1)
                    vec.wait_ge(x_done, OUT_X[name] + m + 1)
                    vec.sem_inc((a_free, b_free)[i], 1)

            def ext_tail(t):
                return t[:, PROMPT:].rearrange("p (b e) -> p b e", b=NSEQ)[:, :, 2:]

            def iteration(t, par_, operands=True, inverse=True, chain=True):
                n, m, j = t + 1, 1 - par_, t - 1
                T = slice(0, TOK)
                copy = nc.vector.tensor_copy
                starts = lambda a: (a[:, 0:PROMPT:C], a[:, PROMPT:TOK:TSAMPLE])
                halves = (slice(0, 64), slice(64, 128))
                chunked = lambda a, r: a[r, :].rearrange("p (c t) -> p c t", c=CHUNKS)
                lev = lambda l, k: con("lev")[:, 128 * l:128 * l + 128].rearrange("p (o w) -> p o w", o=1).broadcast_to([128, k, 128])
                seq9 = lambda r: con("seq")[r, :].rearrange("p (s o) -> p s o", o=1).broadcast_to([64, 9, C])

                def decays():
                    vec.wait_ge(gates_ready, n + 1)
                    for z, d in zip(starts(ZD), starts(DEC)):
                        ins = copy(z, d)
                    link(ins)
                    for d in starts(DEC):
                        ins = nc.vector.memset(d, 0.0)
                    link(ins)
                    if later(n):
                        vec.wait_ge(pend_ready, n)
                    link(nc.vector.tensor_tensor_scan(PPT[:, T], DEC[:, T], ZD, 0.0, ALU.mult, ALU.add))

                    nc.vector.reciprocal(PIN[:, T], PPT[:, T])

                def norms():
                    vec.wait_ge(kkroot, n + 1)
                    link(ts(TC[:, T], TC[:, T], 1e-12, None, ALU.max))
                    link(nc.vector.reciprocal(TC[:, T], TC[:, T]))
                    stt(NKK[:, T], k_all[:, n, :], kk_neg[:, ds(n)], TC[:, T], ALU.mult, ALU.mult)

                def b_rows():
                    vec.wait_ge(kp_ready, n + 1)
                    tt(KP[:, T], KP[:, T], k_all[:, n, :], ALU.mult)
                    link(stt(TA[:, T], TA[:, T], 1.0, NKK[:, T], ALU.add, ALU.mult))
                    for a, r in enumerate(halves):
                        stt(BD[0][r, :, a, :], chunked(TA, r), -0.5, chunked(PIN, r), ALU.mult, ALU.mult)

                def k_rows():
                    for a, r in enumerate(halves):
                        ins = tt(BD[1][r, :, a, :], chunked(KP, r), chunked(PIN, r), ALU.mult)
                    ins.then_inc(bd_ready, 1)
                    stt(TB[:, T], r_all[:, n, :], par("rk", n), KP[:, T], ALU.mult, ALU.mult).then_inc(rkk_ready, 1)

                steps_n = {1: norms, 2: decays, 3: b_rows, 4: k_rows}
                for s_ in range(LV):
                    if chain:
                        vec.wait_ge(out1_mm, CHUNKS * j + s_ + 1)
                        tt(RT.rearrange("p (a t) -> p a t", a=2),
                           bank[0][:, 0:C].rearrange("p (o t) -> p o t", o=1).broadcast_to([128, 2, C]),
                           half.rearrange("p (a o) -> p a o", o=1).broadcast_to([128, 2, C]), ALU.mult).then_inc(rt_ready, 1)
                    tail = s_ < TAIL_LV
                    if inverse:
                        for z in range(2):
                            vec.wait_ge(t1_mm, 2 * LV * t + 2 * s_ + z + 1)
                            k = 3 if z and tail else 2
                            tt(T1[:, 2 * z:2 * z + k, :], bank[2 + z][:, 0:128 * k].rearrange("p (c n) -> p c n", c=k),
                               lev(s_ + 1, k), ALU.mult).then_inc(t1_ready, 1)
                    if operands and s_ in steps_n:
                        steps_n[s_]()
                    if inverse:
                        vec.wait_ge(xup_mm, 2 * LV * t + 2 * s_ + 2)
                        two = lambda o: bank[5][:, o:o + 256].rearrange("p (c n) -> p c n", c=2)
                        if s_ < LV - 1:
                            copy(XM[:, 2:4, :], two(0))
                        copy(XT[par_][:, 2:4, :], two(256)).then_inc(xset_ready[1], 1)
                    if chain and s_ < CHUNKS - 1:
                        vec.wait_ge(s_mm, 4 * j + s_ + 1)
                        pend = PP[m][:, C * s_ + C - 1:C * s_ + C]
                        if s_ == 0:
                            ts(SS, bank[1][:, 256:384], pend, None, ALU.mult).then_inc(s_ready, 1)
                        else:
                            vec.wait_ge(sp_ready, 3 * j + s_)
                            stt(SS, bank[1][:, 256:384], pend, SP, ALU.mult, ALU.add).then_inc(s_ready, 1)
                if chain:
                    vec.wait_ge(sa_ready, CHUNKS * j + CHUNKS)
                    for r in halves:
                        ins = tt(SAX[r, :, :], SA[r, r].rearrange("p (o v) -> p o v", o=1).broadcast_to([64, 9, C]), seq9(r), ALU.mult)
                    ins.then_inc(sax_ready, 1)
                if operands:
                    tt(AR[m][:, 0, 1:TOK], NKK[:, 1:TOK], PPT[:, 0:TOK - 1], ALU.mult)
                    link(tt(AR[m][:, 1, T], r_all[:, n, :], PPT[:, T], ALU.mult))
                    for z, d in zip(starts(AR[m][:, 0, :]), starts(NKK)):
                        ins = copy(z, d)
                    ins.then_inc(ar_ready, 1)
                if chain:
                    vec.wait_ge(fin_mm, j + 1)
                    for r in halves:
                        tt(SOUT[r, 0:8, :], bank[1][r, :].rearrange("p (b v) -> p b v", b=NSEQ), S0[r, :, r], ALU.add)
                        ins = tt(SOUT[r, 8, :], bank[0][r, 0:C], SS[r, r], ALU.add)
                    link(ins)
                    tt(SOUT[:, 0:8, :], SOUT[:, 0:8, :],
                       PP[m][:, PROMPT + TSAMPLE - 1:TOK:TSAMPLE].rearrange("p (b o) -> p b o", o=1).broadcast_to([128, NSEQ, C]), ALU.mult)
                    ts(SOUT[:, 8, :], SOUT[:, 8, :], PP[m][:, PROMPT - 1:PROMPT], None, ALU.mult).then_inc(fin_ready, 1)
                if operands:
                    vec.wait_ge(trans_mm, n + 1)
                    copy(TK[m][2][:, 0:4, :], bank[4].rearrange("p (c n) -> p c n", c=4))
                    for i in range(3):
                        ins = copy(TK[m][i][:, 4, :], bank[5][:, 128 * i:128 * i + 128])
                    ins.then_inc(tok_vec, 1)
                if chain:
                    vec.wait_ge(mean_mm, j + 1)
                    stt(YY, bank[7][:, T], -1.0 / HS, YY, ALU.mult, ALU.add).then_inc(centered, 1)
                if operands:
                    vec.wait_ge(gram_mm, n + 1)
                    for b in range(3):
                        k, tail = (2, "") if b < 2 else (1, "_tail")
                        gr = bank[2 + b][:, 0:256 * k].rearrange("p (c w t) -> p c w t", c=k, w=4)
                        cs = slice(2 * b, 2 * b + k)
                        mask = lambda name, w: con(name + tail).rearrange("p (o w t) -> p o w t", o=1, w=w).broadcast_to([128, k, w, C])
                        tt(STK[m][:, cs, :, :], gr[:, :, 1:4, :], mask("stk", 3), ALU.mult)
                        ins = tt(LT[:, cs, :].rearrange("p c (a t) -> p c a t", a=2),
                                 gr[:, :, 0:1, :].broadcast_to([128, k, 2, C]), mask("lt", 2), ALU.mult)
                    steps.done(ins)
                if chain:
                    vec.wait_ge(var_mm, j + 1)
                    ts(SD, bank[7][:, T], 1.0 / HS, GN_EPS, ALU.mult, ALU.add).then_inc(var_ready, 1)
                if operands:
                    steps.wait()
                    link(tt(LT, LT, ident.rearrange("p (o w) -> p o w", o=1).broadcast_to([128, CHUNKS, 128]), ALU.add))
                    tt(XT[m], LT, lev(0, CHUNKS), ALU.mult).then_inc(xt2_ready, 1)
                if chain:
                    vec.wait_ge(gnroot, j + 1)
                    link(nc.vector.reciprocal(SD, SD))
                    tt(YY, YY, SD, ALU.mult).then_inc(scaled, 1)
                    vec.wait_ge(affine, j + 1)
                    link(tt(YY, YY, BON[m], ALU.add))
                    tt(r_all[:, j, :], YY, GG[m], ALU.mult).then_inc(out_ready, 1)
                if operands:
                    vec.wait_ge(bonus_mm, n + 1)
                    tt(BON[m], bank[6][:, T], v_all[:, n, :], ALU.mult).then_inc(bonus_ready, 1)

            for s_ in (*conv_ready, gated):
                vec.sem_inc(s_, 1)
            nc.vector.memset(ones, 1.0).then_inc(pool_clear, 1)
            vec.wait_ge(in_loaded, 48)
            ts(w0_half, PAR[:, PCOL["w0"]:PCOL["w0"] + KT], 0.5, None, ALU.mult)
            ts(a0_half, PAR[:, PCOL["a0"]:PCOL["a0"] + KT], 0.5, None, ALU.mult)
            ts(ka_half, PAR[:, PCOL["ka"]:PCOL["ka"] + KT], 0.5, None, ALU.mult)
            ts(ka_rest, PAR[:, PCOL["ka"]:PCOL["ka"] + KT], -0.5, 1.0, ALU.mult, ALU.add)
            link(ts(kk_neg, PAR[:, PCOL["kk"]:PCOL["kk"] + KT], -1.0, None, ALU.mult))
            for q in range(4):
                split(0, "pool", q)
            norm_scale(0)
            vec.wait_ge(pst_loaded, 32)
            vec.wait_ge(pool_clear, 2)
            for grp in range(4):
                for k in range(4 * grp, 4 * grp + 4):
                    stt(pext[:, k, POOL_STATE:POOL_STATE + PROMPT], prompt(x[:, k, :]), par("mix0", k), prompt(rnorm), ALU.mult, ALU.mult)
                    ins = stt(ext_samples(pext[:, k, :], POOL_STATE)[:, :, POOL_STATE:], samples(x[:, k, :]),
                              par("mix0", k), samples(rnorm), ALU.mult, ALU.mult)
                link(ins)
                src = pext[:, 4 * grp:4 * grp + 4, :]
                n = 0
                for s in range(grp + 1):
                    d = 1 << s
                    dst = win[s % 2]
                    n += d
                    link(tt(dst[:, :, n:PEXT], src[:, :, n:PEXT], src[:, :, n - d:PEXT - d], ALU.add))
                    src = dst
                hh = pext[:, 4 * grp:4 * grp + 4, :]
                rc = rcnt[:, grp:grp + 1, :].broadcast_to([128, 4, TOK])
                if grp:
                    vec.wait_ge(phi_ready, grp)
                tt(pdiff[:, :, 0:PROMPT], src[:, :, POOL_STATE:POOL_STATE + PROMPT], rc[:, :, 0:PROMPT], ALU.mult)
                for k in range(4):
                    ins = ts(samples(pdiff[:, k, :]), ext_samples(src[:, k, :], POOL_STATE)[:, :, POOL_STATE:],
                             1.0 / WINDOWS[grp], None, ALU.mult)
                link(ins)
                tt(pdiff[:, :, 0:PROMPT], pdiff[:, :, 0:PROMPT], hh[:, :, POOL_STATE:POOL_STATE + PROMPT], ALU.subtract)
                for k in range(4):
                    ins = tt(samples(pdiff[:, k, :]), samples(pdiff[:, k, :]),
                             ext_samples(hh[:, k, :], POOL_STATE)[:, :, POOL_STATE:], ALU.subtract)
                ins.then_inc(pdiff_ready, 1)
                vec.wait_ge(phi_ready, grp + 1)
                vec.wait_ge(pdiff_ready, grp + 1)
                tt(HLO[:, 4 * grp:4 * grp + 4, :], pdiff, HHI[:, 4 * grp:4 * grp + 4, :].bitcast(f32), ALU.subtract)\
                    .then_inc(pooled_ready, 1)
            for g in range(2):
                if g:
                    for q in range(4):
                        split(1, "pool", q)
                for q in range(4):
                    vec.wait_ge(unit_used, 4 * g + q + 1)
                    for i in range(2):
                        m = 8 * g + 2 * q + i
                        stt(x[:, m, :], bank[2 * q + i][:, 0:TOK], par("scale", m), x[:, m, :], ALU.mult, ALU.add)\
                            .then_inc(pool_evac, 1)
                        vec.wait_ge(pool_evac, m + 1)
                        vec.sem_inc(x_done, 1)

            def normed(name):
                return lambda k, i: stt(mix[i], x[:, k, :], par(name, k), rnorm, ALU.mult, ALU.mult)

            prev = None
            for name in NAMES[1:]:
                g0, n = G[name], COUNT[name]
                for q in range(4):
                    split(g0, name, q)
                    if prev and q % 2:
                        evac(prev, g0 - 1, q // 2, COUNT[prev] - 1)
                if name == "in00":
                    norm_scale(1)
                    rest_rows("ffn0", normed("ffn0"), mixed)
                    vec.wait_ge(pool_stored, 16)
                elif name == "in10":
                    norm_scale(3)
                    rest_rows("ffn1", normed("ffn1"), mixed)
                elif name == "lora":
                    norm_scale(2)
                    vec.wait_ge(conv0_stored, 16)
                    vec.wait_ge(shift_loaded, 16)
                    with vec.Fori(0, KT) as k:
                        ins = stt(h[:, k, :], x[:, k, :], par("mix1", k), rnorm, ALU.mult, ALU.mult)
                        ins.then_inc(h0_ready, 1)
                    vec.wait_ge(h0_ready, KT)
                    nc.vector.tensor_copy(shlast[:, :, 0:1], h[:, :, PROMPT - 1:PROMPT])
                    nc.vector.tensor_copy(shlast[:, :, 1:9], h[:, :, PROMPT + TSAMPLE - 1:TOK:TSAMPLE]).then_inc(shlast_ready, 1)
                    tt(xx[:, :, 1:TOK], h[:, :, 0:TOK - 1], h[:, :, 1:TOK], ALU.subtract)
                    ins = ts(xx[:, :, 0], h[:, :, 0], -1.0, None, ALU.mult)
                    link(ins)
                    link(tt(xx[:, :, PROMPT:TOK:TSAMPLE], shprev, h[:, :, PROMPT:TOK:TSAMPLE], ALU.subtract))
                    mix_rows("w")
                    mix_rows("a")
                    for q in range(4):
                        split(g0 + 1, name, q)
                    mix_rows("g")
                elif name == "k":
                    vec.wait_ge(b_free, G["k"] - 2)
                    vec.wait_ge(a_free, G["k"] - 2)
                    ts(hidden[:, 2:4, :], hidden[:, 2:4, :], 0.5, 0.5, ALU.mult, ALU.add).then_inc(hid_ready, 4)
                    mix_rows("k")
                elif name == "r":
                    mix_rows("r")
                elif name == "v":
                    mix_rows("v")
                elif name == "o":
                    vec.wait_ge(chunk_clear, 1)
                    pipeline(iteration, vec.Fori, steps, RSTEPS)
                    rest_rows("o", None, lambda k, i: r_all[:, k, :])
                    vec.wait_ge(refilled, 16)
                if name != "lora":
                    per = 2 if name.startswith("in") else 0
                    if n > 1:
                        with vec.Fori(0, n - 1) as g:
                            steps.enter(g, per)
                            for q in range(4):
                                split(g0 + 1 + g, name, q)
                                if q % 2:
                                    evac(name, g0 + g, q // 2, g)
                        steps.leave(n - 1)
                prev = name
            for i in range(2):
                evac(prev, GROUPS - 1, i, COUNT[prev] - 1)
            norm_scale(4)
            with vec.Fori(0, KT) as k:
                stt(x[:, k, :], x[:, k, :], par("out", k), rnorm, ALU.mult, ALU.mult).then_inc(out_tile, 1)

        @block.gpsimd
        def _(pool):
            steps = Steps(pool, pool_step)

            def square_sums(i):
                if i:
                    pool.wait_ge(sums_done, i)
                steps.done(nc.gpsimd.memset(sumsq, 0.0))
                with pool.Fori(0, KT) as k:
                    steps.enter(k, 2)
                    pool.wait_ge(*((in_loaded, 48) if i == 0 else (x_done, X_BEFORE[i] - KT + k + 1)))
                    steps.wait()
                    steps.done(nc.gpsimd.tensor_tensor(squares, x[:, k, :], x[:, k, :], ALU.mult))
                    steps.wait()
                    steps.done(nc.gpsimd.tensor_tensor(sumsq, sumsq, squares, ALU.add))
                    steps.wait()
                    pool.sem_inc(sq_done, 1)
                steps.leave(KT)

            def mlp_rows(layer):
                if layer == 0:
                    pool.wait_ge(pool_stored, 16)
                pool.wait_ge(ffn_loaded, 32 * (layer + 1))
                for i in range(2):
                    ins = nc.gpsimd.memset(uext[i][:, 0:2], 0.0)
                steps.done(ins)
                steps.wait()
                with pool.Fori(0, FT) as j:
                    n = FT * layer + j
                    for i in range(2):
                        col = FT * i + j
                        pool.wait_ge(conv_ready[i], n + 1)
                        nc.gpsimd.tensor_copy(ext_samples(uext[i], 2)[:, :, 0:2],
                                              prefix[:, ds(col), :].rearrange("p o (b e) -> p (o b) e", b=NSEQ)).then_inc(prefix_set[i], 1)
                        pool.wait_ge(u_ready, 2 * n + i + 1)
                        nc.gpsimd.tensor_copy(ulast[:, ds(col), 0:2], uext[i][:, PROMPT:PROMPT + 2].rearrange("p (o b) -> p o b", o=1))
                        nc.gpsimd.tensor_copy(ulast[:, ds(col), 2:18].rearrange("p o (b e) -> p (o b) e", b=NSEQ),
                                              ext_samples(uext[i], 2)[:, :, 4:6]).then_inc(ulast_saved, 1)

            pool.sem_inc(ulast_saved, 1)
            pool.wait_ge(in_loaded, 48)
            steps.done(nc.gpsimd.memset(pext[:, :, 0:POOL_STATE], 0.0))
            steps.wait()
            pool.sem_inc(pool_clear, 1)
            square_sums(0)
            square_sums(1)
            mlp_rows(0)
            square_sums(2)
            pool.wait_ge(h_ready, H_BEFORE["o"])
            pool.wait_ge(spilled, 16)
            pool.wait_ge(shift_stored, 16)
            for t in (*BD, ZD, *[b[:, TOK:] for b in (TA, PIN, KP)]):
                nc.gpsimd.memset(t, 0.0)
            pool.wait_ge(unit_used, end("v"))
            for b in AR:
                ins = nc.gpsimd.memset(b[:, :, TOK:], 0.0)
            steps.done(ins)
            steps.wait()
            pool.sem_inc(chunk_clear, 1)
            pool.wait_ge(b_free, G["o"] - 2)

            def v_rows(n):
                if later(n):
                    pool.wait_ge(trans_mm, n)
                for a in range(2):
                    r = slice(64 * a, 64 * a + 64)
                    nc.gpsimd.tensor_copy(BD[2][r, 0:4, a, :], v_all[r, n, 0:TAIL].rearrange("p (c t) -> p c t", c=4))
                    ins = nc.gpsimd.tensor_copy(BD[2][r, 4, a, 0:TOK - TAIL], v_all[r, n, TAIL:TOK])
                ins.then_inc(bdv_ready, 1)

            def v_copies(p, i):
                pool.wait_ge(tok_vec, p + 1)
                if later(p):
                    pool.wait_ge(fin_mm, p)
                for a in range(2):
                    r = slice(64 * a, 64 * a + 64)
                    ins = nc.gpsimd.tensor_tensor(
                        VX[r, :, :], TK[i][2][r, CHUNKS - 1, r].rearrange("p (o v) -> p o v", o=1).broadcast_to([64, 9, C]),
                        con("seq")[r, :].rearrange("p (s o) -> p s o", o=1).broadcast_to([64, 9, C]), ALU.mult)
                ins.then_inc(vx_ready, 1)

            v_rows(0)
            v_rows(1)
            v_copies(0, 0)
            with pool.Fori(0, PAIRS // 2 - 1) as g:
                for i in range(2):
                    v_rows(2 * g + (2 + i))
                    v_copies(2 * g + (1 + i), 1 - i)
            v_copies(PAIRS - 1, 1)
            pool.wait_ge(vx_ready, PAIRS)
            pool.wait_ge(out_ready, PAIRS)
            square_sums(3)
            mlp_rows(1)
            square_sums(4)


def lay_out(v):
    f = {n: np.asarray(a) for n, a in v.items()}

    def feat(a):
        a = np.moveaxis(a, -1, 0)
        return np.ascontiguousarray(np.moveaxis(a.reshape(KT, 128, *a.shape[1:]), 0, 1))

    def columns(w):
        k, m = w.shape
        return w.reshape(k // 128, 128, m // 128, 128).transpose(2, 1, 0, 3)

    def widened(w):
        return np.concatenate([w, np.zeros((w.shape[0], 128 - w.shape[1]), w.dtype)], 1)

    units = np.zeros((4 * GROUPS, 128, 8, 128), np.float32)

    def place(name, cols):
        u = 4 * FIRST[name]
        k = cols.shape[2]
        n = cols.shape[0]
        units[u:u + 2 * n:2] = cols[:, :, 0:8]
        units[u + 1:u + 2 * n:2, :, 0:k - 8] = cols[:, :, 8:]

    pw = f["pool_w"][0]
    for grp in range(4):
        c = columns(pw[grp])
        units[2 * grp:2 * grp + 2] = c.reshape(2, 2, 128, 4, 128).transpose(0, 2, 1, 3, 4).reshape(2, 128, 8, 128)
    for l in range(LAYERS):
        cin, cout = columns(f["ffn_w_in"][l]), columns(f["ffn_w_out"][l])
        for s, n in enumerate(SEGS):
            a = SEG0[s]
            both = np.stack([cin[a:a + n], cin[FT + a:FT + a + n]], 1).reshape(2 * n, 128, KT, 128)
            place(f"in{l}{s}", both)
            place(f"out{l}{s}", cout[:, :, a:a + n])
    place("lora", columns(np.concatenate([widened(f["rwkv_w1"][0]), widened(f["rwkv_a1"][0]), f["rwkv_g1"][0]], 1)))
    for name, w in (("k", "rwkv_wk"), ("r", "rwkv_wr"), ("v", "rwkv_wv"), ("o", "rwkv_wo")):
        place(name, columns(f[w][0]))
    l2 = np.zeros((PAIRS, 128, 4, 128), np.float32)
    l2[:, 0:LORA, 0] = f["rwkv_w2"][0].reshape(LORA, PAIRS, 128).transpose(1, 0, 2)
    l2[:, 0:LORA, 1] = f["rwkv_a2"][0].reshape(LORA, PAIRS, 128).transpose(1, 0, 2)
    l2[:, :, 2:4] = f["rwkv_g2"][0].reshape(2, 128, PAIRS, 128).transpose(2, 1, 0, 3)
    rows = np.concatenate([f["meta_tokens"], f["x_prompt"][0], f["x_sample"].reshape(-1, D)], 0)
    vecs = [f["norm_mix"][0], f["norm_ffn"][0], f["norm_mix"][1], f["norm_ffn"][1], f["norm_out"], f["pool_scale"][0],
            *f["rwkv_mu"][0], f["rwkv_w0"][0], f["rwkv_a0"][0], f["rwkv_kk"][0], f["rwkv_ka"][0],
            f["rwkv_lnw"][0], f["rwkv_lnb"][0], f["rwkv_rk"][0].reshape(-1)]
    par = np.stack(vecs).reshape(len(vecs), KT, 128).transpose(2, 0, 1).reshape(128, NPAR)
    fp = np.concatenate([f["ffn_conv_w"], f["ffn_conv_b"][:, None]], 1)
    fp = fp.reshape(LAYERS, 4, 2 * FT, 128).transpose(0, 3, 2, 1)
    cst = f["state_ffn_conv"].reshape(LAYERS, NSEQ * 2, 2 * FT, 128).transpose(0, 3, 2, 1)
    s = f["state_rwkv_wkv"][0].reshape(NSEQ, PAIRS, 2, HS, HS)
    wkv = np.zeros((PAIRS, 2, HS, NSEQ, 2, HS), np.float32)
    for a in range(2):
        wkv[:, a, :, :, a, :] = s[:, :, a].transpose(1, 3, 0, 2)
    c = np.ascontiguousarray
    return {
        "W_all": units.reshape(4 * GROUPS, 128, 1024), "L2_all": l2.reshape(PAIRS, 128, 512), "xT": feat(rows),
        "params": c(par), "ffnpar": c(fp), "consts": constants(),
        "pool_st": feat(np.concatenate([f["state_pool"][0], np.zeros((NSEQ, TSAMPLE, D), np.float32)], 1)).reshape(128, KT, -1),
        "shift_st": feat(f["state_rwkv_shift"][0]), "wkv_st": wkv.reshape(PAIRS, 128, NSEQ * 128), "conv_st": c(cst),
    }


OUTPUTS = {"yT": (128, KT, TOK), "pool_out": (128, KT, PEXT - PROMPT), "shift_out": (128, KT, 9),
           "wkv_out": (PAIRS, 128, 9 * C), "conv_out": (LAYERS, 128, 2 * FT, 18)}
INPUTS = ["W_all", "L2_all", "xT", "params", "ffnpar", "consts", "pool_st", "shift_st", "wkv_st", "conv_st"]


def kernel(**inputs):
    import concourse.bacc as _bacc
    from concourse import mybir as _mybir
    from concourse.bass_utils import run_bass_kernel_spmd as _run

    arrays = lay_out(inputs)
    nc = _bacc.Bacc("TRN2", target_bir_lowering=False, num_devices=1)
    f32 = _mybir.dt.float32
    ins = [nc.dram_tensor(n, arrays[n].shape, f32, kind="ExternalInput").ap() for n in INPUTS]
    outs = [nc.dram_tensor(n, s, f32, kind="ExternalOutput").ap() for n, s in OUTPUTS.items()]
    spill = nc.dram_tensor("x_spill", (128, KT, TOK), f32, kind="Internal").ap()
    build(nc, *ins, *outs, spill)
    r = _run(nc, [arrays], core_ids=[0]).results[0]

    def rows(a):
        return np.ascontiguousarray(a.transpose(2, 1, 0).reshape(a.shape[2], D))

    y = rows(r["yT"])
    pool, shift = rows(r["pool_out"]), rows(r["shift_out"])
    w = r["wkv_out"].reshape(PAIRS, 2, HS, 9, HS).transpose(3, 0, 1, 4, 2).reshape(9, HEADS, HS, HS)
    cv = r["conv_out"].transpose(0, 3, 2, 1).reshape(LAYERS, 18, 2 * D_FF)
    c = np.ascontiguousarray
    return (c(y[N_META:PROMPT][None]), c(y[PROMPT:].reshape(NSEQ, TSAMPLE, D)),
            c(pool[None, None, 0:15]), c(pool[15:].reshape(1, NSEQ, 15 + TSAMPLE, D)[:, :, TSAMPLE:]),
            c(shift[None, 0:1]), c(shift[None, 1:9]),
            c(w[8][None, None]), c(w[0:8][None]),
            c(cv[:, None, 0:2]), c(cv[:, 2:18].reshape(LAYERS, NSEQ, 2, 2 * D_FF)))
```

```python
import numpy as np

import concourse.bass as bass
from concourse import mybir

D = 2048
N_META, SEQ = 16, 256
PROMPT = N_META + SEQ
NSEQ, TSAMPLE = 8, 4
TOK = PROMPT + NSEQ * TSAMPLE
KT = D // 128
D_FF = 5504
FT = D_FF // 128
LAYERS = 2
POOL_STATE = 15
WINDOWS = (2, 4, 8, 16)
HEADS, HS = 32, 64
PAIRS = HEADS // 2
C = 64
CHUNKS = 5
PADTOK = C * CHUNKS
TAIL = 4 * C
TAILP = PROMPT - TAIL
EXT = 2 + PROMPT + NSEQ * (2 + TSAMPLE)
CONVW = EXT - 2
PEXT = POOL_STATE + PROMPT + NSEQ * (POOL_STATE + TSAMPLE)
PS0 = POOL_STATE + PROMPT
NORM_EPS = 1e-6
GN_EPS = 64e-5
LORA = 96
RSTEPS = 10
DECAY_SCALE = -float(np.exp(-0.5))

SEGS = (16, 16, 11)
SEG0 = (0, 16, 32)
PHASES = [("pool", 2, (8, 8, 8, 8))]


def _ffn_phases(layer):
    for s, n in enumerate(SEGS):
        PHASES.append((f"in{layer}{s}", n, (8, 8, 8, 8)))
        PHASES.append((f"out{layer}{s}", 8, (8, n - 8, 8, n - 8)))


_ffn_phases(0)
PHASES += [("lora", 2, (8, 8, 8, 8)), ("k", 8, (8, 8, 8, 8)), ("r", 8, (8, 8, 8, 8)),
           ("v", 8, (8, 8, 8, 8)), ("o", 8, (8, 8, 8, 8))]
_ffn_phases(1)
FIRST, COUNT = {}, {}
_g = 0
for _n, _c, _s in PHASES:
    FIRST[_n], COUNT[_n] = _g, _c
    _g += _c
GROUPS = _g

PCOL = {n: 16 * i for i, n in enumerate(
    ["mix0", "ffn0", "mix1", "ffn1", "out", "scale", "mu0", "mu1", "mu2", "mu3", "mu4", "mu5",
     "w0", "a0", "kk", "ka", "lnw", "lnb", "rk"])}
NPAR = 16 * len(PCOL)

CCOL, _at = {}, 0
for _n, _w in [("ident", 128), ("bones", 128), ("half", 2), ("stk", 192), ("stk_tail", 192),
               ("lt", 128), ("lt_tail", 128), ("lev", 6 * 128), ("seq", 9), ("rcnt", 4 * TOK)]:
    CCOL[_n] = (_at, _w)
    _at += _w
NCON = _at
NRES = CCOL["rcnt"][0]


def constants():
    out = np.zeros((128, NCON), np.float32)

    def put(name, a):
        at, w = CCOL[name]
        out[:, at:at + w] = np.asarray(a, np.float32).reshape(128, w)

    p = np.arange(128)
    head, row = p // 64, p % 64
    put("ident", np.eye(128))
    put("bones", head[:, None] == head[None, :])
    put("half", head[:, None] == np.arange(2)[None, :])
    t = np.arange(64)
    seq = np.where(t < TAILP, 8, np.minimum((t - TAILP) // TSAMPLE, 7))
    dead = t >= TAILP + NSEQ * TSAMPLE
    for tail in (False, True):
        same = (seq[row][:, None] == seq[None, :]) & ~dead[row][:, None] & ~dead[None, :] if tail else np.ones((128, 64), bool)
        strict = same & (row[:, None] < t[None, :])
        upto = same & (row[:, None] <= t[None, :])
        suffix = "_tail" if tail else ""
        put("stk" + suffix, np.concatenate([upto, strict, upto], 1))
        put("lt" + suffix, np.concatenate([strict * (head == 0)[:, None], strict * (head == 1)[:, None]], 1))
    lev = []
    for l in range(6):
        m = 1 << l
        block = (p[:, None] // (2 * m)) == (p[None, :] // (2 * m))
        low = block & (p[:, None] % (2 * m) >= m) & (p[None, :] % (2 * m) < m)
        lev.append((low.T if l == 0 else low) + np.eye(128))
    put("lev", np.concatenate(lev, 1))
    put("seq", (seq[row][:, None] == np.arange(9)[None, :]) & ~dead[row][:, None])
    tok = np.arange(TOK)
    cnt = np.stack([np.where(tok < PROMPT, np.minimum(w, tok + 1), w) for w in WINDOWS])
    put("rcnt", np.tile((np.float32(1) / cnt.astype(np.float32)).reshape(1, -1), (128, 1)))
    return out


def ds(i, n=1):
    return slice(i, i + n) if isinstance(i, int) else bass.ds(i, n)


class Steps:

    def __init__(self, eng, sem):
        self.eng, self.sem, self.base, self.off = eng, sem, 0, 0

    def done(self, ins):
        ins.then_inc(self.sem, 1)
        self.off += 1
        return ins

    def wait(self):
        self.eng.wait_ge(self.sem, self.base + self.off)

    def enter(self, i, per):
        self.start, self.per = self.base + self.off, per
        self.base, self.off = self.start + per * i, 0

    def leave(self, count):
        assert self.off == self.per, (self.off, self.per)
        self.base, self.off = self.start + self.per * count, 0




def build(nc, W_all, L2_all, xT, params, ffnpar, consts, pool_st, shift_st, wkv_st, conv_st,
          yT, pool_out, shift_out, wkv_out, conv_out, x_spill):
    f32, f32r = mybir.dt.float32, mybir.dt.float32r
    ALU, ACT = mybir.AluOpType, mybir.ActivationFunctionType

    top = [(nc.sbuf_base + 63) // 64 * 64]

    def sb(name, shape, dt=f32, at=None):
        ptr = top if at is None else at
        t = nc.alloc_sbuf_tensor_at(name, shape, dt, offset=ptr[0]).ap()
        ptr[0] += (4 * int(np.prod(shape[1:])) + 31) // 32 * 32
        assert ptr[0] <= nc.sbuf_usable_end, (name, ptr[0])
        return t

    RAW = [sb(f"raw{q}", [128, 8 * 128]) for q in range(4)]
    WHI = [sb(f"whi{q}", [128, 8 * 128], f32r) for q in range(4)]
    WLO = [sb(f"wlo{q}", [128, 8 * 128], f32r) for q in range(4)]
    at_hh = list(top)
    pdiff_all = sb("pdiff", [128, KT, TOK], at=list(top))
    HHI = sb("h_hi", [128, KT, TOK], f32r)
    HLO = sb("h_lo", [128, KT, TOK], f32r)
    PAR = sb("par", [128, NPAR])
    CON = sb("con", [128, NRES])
    w0_half, a0_half, ka_half, ka_rest, kk_neg = [
        sb(n, [128, KT]) for n in ("w0_half", "a0_half", "ka_half", "ka_rest", "kk_neg")]
    at_sq = list(top)
    squares, sumsq, meansq, rnorm = [sb(n, [128, TOK]) for n in ("squares", "sumsq", "meansq", "rnorm")]
    ones = sb("ones", [128, 128])
    at_mix = list(top)
    mix = [sb(f"mix{i}", [128, TOK]) for i in range(4)]
    at_x = list(top)
    at_x0 = at_x[0]
    x = sb("x", [128, KT, TOK])
    at = list(top)
    pext = sb("pext", [128, KT, PEXT], at=at)
    win = [sb(f"win{i}", [128, 4, PEXT], at=at) for i in range(5)]
    rcnt = sb("rcnt", [128, 4, TOK], at=at)
    at = list(top)
    AHI = sb("act_hi", [128, 16, TOK], f32r, at=at)
    ALO = sb("act_lo", [128, 16, TOK], f32r, at=at)
    uext = [sb(f"uext{i}", [128, EXT], at=at) for i in range(2)]
    conv = [sb(f"conv{i}", [128, CONVW], at=at) for i in range(2)]
    sgate = sb("sgate", [128, CONVW], at=at)
    act_f = sb("act_f", [128, TOK], at=at)
    prefix = sb("prefix", [128, 2 * FT, 16], at=at)
    ulast = sb("ulast", [128, 2 * FT, 18], at=at)
    fpar = sb("fpar", [128, 2 * FT, 4], at=at)
    at = list(top)
    k_all = sb("k_all", [128, KT, TOK], at=at)
    r_all = sb("r_all", [128, KT, TOK], at=at)
    hidden = sb("hidden", [128, 4, TOK], at=at)
    at_h = list(at)
    h = sb("h", [128, KT, TOK], at=at)
    xx = sb("xx", [128, KT, TOK], at=at)
    shprev = sb("shift_prev", [128, KT, NSEQ], at=at)
    shlast = sb("shift_last", [128, KT, 9], at=at)
    v_all = sb("v_all", [128, KT, TOK], at=at_h)
    AR = [sb(f"ar{i}", [128, 2, PADTOK], at=at_hh) for i in range(2)]
    TK = [[sb(f"tok_{n}{i}", [128, CHUNKS, 128], at=at_hh) for n in "bkv"] for i in range(2)]
    STK = [sb(f"stk{i}", [128, CHUNKS, 3, C], at=at_hh) for i in range(2)]
    XT = [sb(f"xt{i}", [128, CHUNKS, 128], at=at_hh) for i in range(2)]
    PP = [sb(f"pprod{i}", [128, TOK], at=at_hh) for i in range(2)]
    RT, RHS, SS, SP = [sb(n, [128, 128], at=at_hh) for n in ("rt", "rhs", "ss", "sp")]
    assert at_hh[0] <= at_sq[0]
    DEC, NKK, PIN, TA, TB, TC, KP, PPT = [
        sb(n, [128, PADTOK], at=at_x) for n in ("decay", "nkk", "pinv", "ta", "tb", "tc", "kp", "ppt")]
    SOUT = sb("sout", [128, 9, C], at=at_x)
    SA = sb("sa", [128, 128], at=at_x)
    assert at_x[0] <= top[0]
    BD = [sb(n, [128, CHUNKS, 2, C], at=at_h) for n in ("bd_b", "bd_k", "bd_v")]
    LT = sb("lt", [128, CHUNKS, 128], at=at_h)
    XM = sb("xm", [128, CHUNKS, 128], at=at_h)
    T1 = sb("t1", [128, CHUNKS, 128], at=at_h)
    S0 = sb("s0bd", [128, NSEQ, 128], at=at_h)
    L2 = [sb(f"l2_{i}", [128, 4 * 128], at=at_h) for i in range(2)]
    SAX, VX = sb("sax", [128, 9, C], at=at_mix), sb("vx", [128, 9, C], at=at_mix)
    assert at_mix[0] <= at_x0
    YY0, SQ, SD, ZD = [sb(n, [128, TOK], at=at_sq) for n in ("yy0", "ysq", "ysd", "restart")]
    YY = [YY0, sb("yy1", [128, TOK], at=at_x)]
    assert at_x[0] <= top[0]

    bank = [nc.alloc_psum_tensor(f"bank{i}", [128, 512], f32).ap() for i in range(8)]

    def con(name):
        at_, w = CCOL[name]
        return CON[:, at_:at_ + w]

    def par(name, m):
        return PAR[:, ds(PCOL[name] + m)]

    ident, bones = con("ident"), con("bones")
    half = con("half")
    TRANSPOSE, mm_ = nc.tensor.transpose, nc.tensor.matmul

    def sem(name):
        return nc.alloc_semaphore(name)

    raw_loaded = [sem(f"raw_loaded{q}") for q in range(4)]
    (whi_ready, wlo_ready, unit_used, a_free, b_free, in_loaded, pst_loaded, ffn_loaded, shift_loaded,
     pool_stored, conv0_stored, shift_stored, stored, x_done, sq_done, sums_done, ms_done, root_done,
     mix_ready, hhi_ready, h_ready, h0_ready, pdiff_ready, pool_evac,
     pool_clear, u_ready, c0_ready, silu_ready, gated, acthi_ready, act_ready, ulast_saved,
     hid_ready, spilled, refilled, s0_loaded, chunk_clear, out_tile, shlast_ready) = [
        sem(n) for n in """whi_ready wlo_ready unit_used a_free b_free in_loaded pst_loaded ffn_loaded
        shift_loaded pool_stored conv0_stored shift_stored stored x_done sq_done sums_done ms_done root_done
        mix_ready hhi_ready h_ready h0_ready pdiff_ready pool_evac
        pool_clear u_ready c0_ready silu_ready gated acthi_ready act_ready ulast_saved
        hid_ready spilled refilled s0_loaded chunk_clear out_tile shlast_ready""".split()]
    ones_set, xx_ready = sem("ones_set"), sem("xx_ready")
    x_loaded = [sem(f"x_loaded{i}") for i in range(4)]
    squared, sq_used, pooled_norm, win_ready = [sem(n) for n in ("squared", "sq_used", "pooled_norm", "win_ready")]
    prefix_set = [sem(f"prefix_set{i}") for i in range(2)]
    conv_ready = [sem(f"conv_ready{i}") for i in range(2)]
    l2_loaded = [sem(f"l2_loaded{i}") for i in range(2)]
    vec_step, act_step, pool_step = sem("vec_step"), sem("act_step"), sem("pool_step")
    RSEMS = """lora_mm gate_mm kksum_mm bonus_mm trans_mm gram_mm gates_ready kp_ready kksq_ready kkroot
        bd_ready bdv_ready ar_ready rkk_ready bonus_ready gg_ready tok_act tok_vec pend_ready xt2_ready x2_mm
        x2_ready t1_mm t1_ready xup_mm xtail_mm xtail_ready z_mm out1_mm rt_ready rhs_mm rhs_ready sa_mm sa_ready
        y_mm s_mm sp_ready s_ready y_ready sax_ready vx_ready fin_mm fin_ready mean_mm centered ycsq_ready gram_b_mm sout_ready stk_ready trans_bk_mm grams_left
        var_mm var_ready gnroot scaled affine out_ready wkv_stored""".split()
    (lora_mm, gate_mm, kksum_mm, bonus_mm, trans_mm, gram_mm, gates_ready, kp_ready, kksq_ready, kkroot,
     bd_ready, bdv_ready, ar_ready, rkk_ready, bonus_ready, gg_ready, tok_act, tok_vec, pend_ready, xt2_ready, x2_mm,
     x2_ready, t1_mm, t1_ready, xup_mm, xtail_mm, xtail_ready, z_mm, out1_mm, rt_ready, rhs_mm, rhs_ready, sa_mm, sa_ready,
     y_mm, s_mm, sp_ready, s_ready, y_ready, sax_ready, vx_ready, fin_mm, fin_ready, mean_mm, centered, ycsq_ready, gram_b_mm, sout_ready, stk_ready, trans_bk_mm, grams_left,
     var_mm, var_ready, gnroot, scaled, affine, out_ready, wkv_stored) = [sem(n) for n in RSEMS]
    xset_ready = [sem(f"xset_ready{z}") for z in range(2)]

    LV = 5
    TAIL_LV = 3
    X_BEFORE = [0, 16, 64, 80, 128]
    OUT_X = {"out00": 16, "out01": 32, "out02": 48, "o": 64, "out10": 80, "out11": 96, "out12": 112}
    H_BEFORE = {"ffn0": 0, "mu1": 16, "mu4": 32, "mu5": 48, "mu2": 64, "mu0": 80, "mu3": 96, "o": 112, "ffn1": 128}
    MADE_BEFORE = {n: min(c, 112) for n, c in H_BEFORE.items() if n != "o"}
    MIXES = {"w": "mu1", "a": "mu4", "g": "mu5", "k": "mu2", "r": "mu0", "v": "mu3"}
    XX_SPLIT = 10

    def shifted(tt, ts, link, k0, k1):
        k = slice(k0, k1)
        tt(xx[:, k, 1:TOK], h[:, k, 0:TOK - 1], h[:, k, 1:TOK], ALU.subtract)
        link(ts(xx[:, k, 0], h[:, k, 0], -1.0, None, ALU.mult))
        link(tt(xx[:, k, PROMPT:TOK:TSAMPLE], shprev[:, k, :], h[:, k, PROMPT:TOK:TSAMPLE], ALU.subtract))

    def windows(tt, grp, bufs, link):
        src, n = pext[:, 4 * grp:4 * grp + 4, :], 0
        for s in range(grp + 1):
            d = 1 << s
            dst = bufs[s % 2]
            n += d
            link(tt(dst[:, :, n:PEXT], src[:, :, n:PEXT], src[:, :, n - d:PEXT - d], ALU.add))
            src = dst
        return src

    def later(n):
        return not isinstance(n, int) or n > 0

    def pipeline(iteration, loop, steps=None, per=0):
        iteration(-1, 1, inverse=False, chain=False, finish=False)
        iteration(0, 0, chain=False, finish=False)
        iteration(1, 1, finish=False)
        with loop(0, PAIRS // 2 - 2) as g:
            if steps:
                steps.enter(g, 2 * per)
            iteration(2 * g + 2, 0)
            iteration(2 * g + 3, 1)
        if steps:
            steps.leave(PAIRS // 2 - 2)
        iteration(PAIRS - 2, 0)
        iteration(PAIRS - 1, 1, operands=False)
        iteration(PAIRS, 0, operands=False, inverse=False)
        iteration(PAIRS + 1, 1, operands=False, inverse=False, chain=False)

    SIZES = {n: s for n, _, s in PHASES}
    NAMES = [n for n, _, _ in PHASES]
    G = FIRST

    def end(name):
        return 4 * (FIRST[name] + COUNT[name])

    def prompt(t):
        return t[..., 0:PROMPT]

    def samples(t):
        return t[:, PROMPT:TOK].rearrange("p (b e) -> p b e", b=NSEQ)

    def ext_samples(t, n):
        return t[:, n + PROMPT:].rearrange("p (b e) -> p b e", b=NSEQ)

    def flat(bd, c):
        return bd[:, c, :, :].rearrange("p a b -> p (a b)")

    with nc.Block() as block:

        @block.sync
        def _(sp):
            def load_group(G_, name, behind=wlo_ready):
                sizes = SIZES[name]
                for q in range(4):
                    if behind is not None:
                        sp.wait_ge(behind, 4 * G_ + (q - 3))
                    sp.dma_start(RAW[q][:, 0:sizes[q] * 128], W_all[4 * G_ + q, :, 0:sizes[q] * 128])\
                        .then_inc(raw_loaded[q], 16)

            def load_rest(name, first=1):
                with sp.Fori(0, COUNT[name] - first) as g:
                    load_group(G[name] + first + g, name)

            def load_mlp(layer):
                sp.dma_start(prefix, conv_st[layer]).then_inc(ffn_loaded, 16)
                sp.dma_start(fpar, ffnpar[layer]).then_inc(ffn_loaded, 16)

            for i in range(4):
                sp.dma_start(x[:, 4 * i:4 * i + 4, :], xT[:, 4 * i:4 * i + 4, :]).then_inc(x_loaded[i], 16)
            sp.dma_start(PAR, params).then_inc(in_loaded, 16)
            sp.dma_start(CON, consts[:, 0:NRES]).then_inc(in_loaded, 16)
            sp.dma_start(rcnt, consts[:, NRES:].rearrange("p (g t) -> p g t", g=4)).then_inc(pst_loaded, 16)
            sp.dma_start(pext[:, :, POOL_STATE + PROMPT:], pool_st).then_inc(pst_loaded, 16)
            load_group(0, "pool", None)
            load_group(1, "pool", unit_used)

            def mlp_loads(layer):
                first = f"in{layer}0"
                load_group(G[first], first, wlo_ready if layer else unit_used)
                if layer == 0:
                    sp.wait_ge(pdiff_ready, 4)
                    sp.dma_start(pool_out, pext[:, :, PROMPT:]).then_inc(pool_stored, 16)
                    sp.wait_ge(pool_stored, 16)
                    sp.wait_ge(unit_used, end("pool"))
                else:
                    sp.wait_ge(x_done, X_BEFORE[3])
                    sp.wait_ge(wkv_stored, 16 * PAIRS)
                load_mlp(layer)
                load_rest(first)
                for s in range(3):
                    if s:
                        load_rest(f"in{layer}{s}", 0)
                    load_rest(f"out{layer}{s}", 0)

            mlp_loads(0)
            load_group(G["lora"], "lora")
            sp.wait_ge(ulast_saved, 2 * FT + 1)
            sp.dma_start(conv_out[0], ulast).then_inc(conv0_stored, 16)
            sp.wait_ge(conv0_stored, 16)
            sp.dma_start(shprev, shift_st).then_inc(shift_loaded, 16)
            load_rest("lora")
            load_rest("k", 0)
            load_rest("r", 0)
            load_rest("v", 0)
            load_group(G["o"], "o")
            sp.wait_ge(shlast_ready, 1)
            sp.dma_start(shift_out, shlast).then_inc(shift_stored, 16)
            sp.dma_start(x_spill, x).then_inc(spilled, 16)
            sp.wait_ge(chunk_clear, 1)
            for i in range(2):
                sp.dma_start(L2[i], L2_all[i]).then_inc(l2_loaded[i], 16)
            sp.dma_start(S0, wkv_st[0].rearrange("p (b n) -> p b n", b=NSEQ)).then_inc(s0_loaded, 16)

            sp.wait_ge(gg_ready, 1)
            sp.dma_start(L2[0], L2_all[2]).then_inc(l2_loaded[0], 16)

            def pair_io(p, i, weights=True, states=True):
                sp.wait_ge(fin_ready, p)
                sp.dma_start(wkv_out[p - 1].rearrange("p (b n) -> p b n", b=9), SOUT).then_inc(wkv_stored, 16)
                if weights:
                    sp.wait_ge(gg_ready, p + 1)
                    sp.dma_start(L2[i], L2_all[p + 2]).then_inc(l2_loaded[i], 16)
                sp.wait_ge(wkv_stored, 16 * p)
                if states:
                    sp.dma_start(S0, wkv_st[p].rearrange("p (b n) -> p b n", b=NSEQ)).then_inc(s0_loaded, 16)

            with sp.Fori(0, PAIRS // 2 - 2) as g:
                pair_io(2 * g + 1, 1)
                pair_io(2 * g + 2, 0)
            pair_io(PAIRS - 3, 1)
            pair_io(PAIRS - 2, 0, weights=False)
            pair_io(PAIRS - 1, 1, weights=False)
            pair_io(PAIRS, 0, weights=False, states=False)
            sp.wait_ge(out_ready, PAIRS)
            sp.dma_start(x, x_spill).then_inc(refilled, 16)
            load_rest("o")
            mlp_loads(1)
            sp.wait_ge(ulast_saved, 4 * FT + 1)
            sp.dma_start(conv_out[1], ulast).then_inc(stored, 16)
            with sp.Fori(0, KT // 2) as k:
                sp.wait_ge(out_tile, 2 * k + 2)
                sp.dma_start(yT[:, ds(2 * k, 2), :], x[:, ds(2 * k, 2), :]).then_inc(stored, 16)
            sp.wait_ge(stored, 16 * (KT // 2 + 1))
            sp.wait_ge(shift_stored, 16)

        @block.tensor
        def _(pe):
            def three(acc, wh, wl, xh, xl, first, last):
                mm_(acc, wh, xh, start=first, stop=False)
                mm_(acc, wh, xl, start=False, stop=False)
                return mm_(acc, wl, xh, start=False, stop=last)

            def accumulate(G_, ab, name, hi, lo, free=True, rows=None):
                sizes = SIZES[name][2 * ab:2 * ab + 2]
                for i in range(2):
                    q = 2 * ab + i
                    pe.wait_ge(wlo_ready, 4 * G_ + (q + 1))
                    if i == 0 and free:
                        pe.wait_ge((a_free, b_free)[ab], G_ - 2)
                    for j in range(sizes[i]):
                        k = 8 * i + j
                        if rows is not None:
                            pe.wait_ge(rows[0], rows[1] + k + 1)
                        w = slice(128 * j, 128 * j + 128)
                        mm = three(bank[ab][:, 0:TOK], WHI[q][:, w], WLO[q][:, w], hi[:, k, :], lo[:, k, :],
                                   k == 0, k == sum(sizes) - 1)
                    mm.then_inc(unit_used, 1)

            def both(G_, hi, lo, rows):
                pe.wait_ge(wlo_ready, 4 * G_ + 3)
                if G_ > 2:
                    pe.wait_ge(a_free, G_ - 2)
                    pe.wait_ge(b_free, G_ - 2)
                for k in range(KT):
                    if k == 8:
                        pe.wait_ge(wlo_ready, 4 * G_ + 4)
                    pe.wait_ge(rows[0], rows[1] + k + 1)
                    for ab in range(2):
                        q, w = 2 * ab + k // 8, slice(128 * (k % 8), 128 * (k % 8) + 128)
                        mm = three(bank[ab][:, 0:TOK], WHI[q][:, w], WLO[q][:, w], hi[:, k, :], lo[:, k, :],
                                   k == 0, k == KT - 1)
                        if k == 7 and ab == 0:
                            mm.then_inc(unit_used, 1)
                        if k == KT - 1:
                            mm.then_inc(unit_used, 1 + ab)

            def run(name, hi, lo, rows=None, start=0):
                if rows is not None and rows[0] is h_ready:
                    both(G[name], hi, lo, rows)
                    start = 1
                elif rows is not None:
                    accumulate(G[name], 0, name, hi, lo, rows=rows)
                    accumulate(G[name], 1, name, hi, lo)
                    start = 1
                with pe.Fori(0, COUNT[name] - start) as g:
                    for ab in range(2):
                        accumulate(G[name] + start + g, ab, name, hi, lo)

            def norm_sum(i):
                pe.wait_ge(sq_done, KT * i)
                mm_(bank[7][:, 0:TOK], ones, sumsq, start=True, stop=True).then_inc(sums_done, 1)

            pe.wait_ge(ones_set, 1)
            for k in range(KT):
                pe.wait_ge(squared, k + 1)
                mm_(bank[7][:, 0:TOK], ones, mix[k % 4], start=k == 0, stop=k == KT - 1).then_inc(sq_used, 1)
            pe.wait_ge(in_loaded, 32)
            for g in range(2):
                for q in range(4):
                    grp = 2 * g + q // 2
                    pe.wait_ge(raw_loaded[q], 16 * g + 16)
                    pe.wait_ge(pdiff_ready, grp + 1)
                    if g:
                        pe.wait_ge(pool_evac, 2 * q + 2)
                    for i in range(2):
                        for c in range(4):
                            w = slice(128 * (4 * i + c), 128 * (4 * i + c) + 128)
                            k = 4 * grp + c
                            if g == 0 and q == 3 and i == 1 and c == 0:
                                pe.wait_ge(ms_done, 1)
                            mm = mm_(bank[2 * q + i][:, 0:TOK], RAW[q][:, w], pdiff_all[:, k, :], start=c == 0, stop=c == 3)
                    mm.then_inc(unit_used, 1)
            pe.wait_ge(pool_evac, 16)

            def mlp(layer):
                norm_sum(1 + 2 * layer)
                for s in range(3):
                    run(f"in{layer}{s}", HHI, HLO, (h_ready, H_BEFORE[f"ffn{layer}"]) if s == 0 else None)
                    run(f"out{layer}{s}", AHI, ALO, (act_ready, FT * layer + SEG0[s]))

            mlp(0)
            norm_sum(2)
            for i, m in enumerate("wa"):
                accumulate(G["lora"], i, "lora", HHI, HLO, rows=(h_ready, H_BEFORE[MIXES[m]]))
            both(G["lora"] + 1, HHI, HLO, (h_ready, H_BEFORE["mu5"]))
            run("k", HHI, HLO, (h_ready, H_BEFORE["mu2"]))
            run("r", HHI, HLO, (h_ready, H_BEFORE["mu0"]))

            def iteration(t, par, operands=True, inverse=True, chain=True, finish=True):
                n, m, j = t + 1, 1 - par, t - 1
                cols = lambda c: slice(128 * (c % 4), 128 * (c % 4) + 128)

                def t1_products(l, z):
                    cs = [2 * z, 2 * z + 1]
                    if l:
                        pe.wait_ge(xset_ready[z], LV * t + l)
                    else:
                        pe.wait_ge(grams_left, t + 1)
                        pe.wait_ge(x2_ready, 2 * t + z + 1)
                    if z and l < TAIL_LV:
                        cs.append(CHUNKS - 1)
                        if l:
                            pe.wait_ge(xtail_ready, TAIL_LV * t + l)
                    for i, c in enumerate(cs):
                        mm = mm_(bank[2 + z][:, cols(i)], LT[:, c, :], XM[:, c, :], start=True, stop=True)
                    mm.then_inc(t1_mm, 1)

                def update_products(l, z):
                    cs = [2 * z, 2 * z + 1] if z < 2 else [CHUNKS - 1]
                    if z == 2 and l == 0:
                        pe.wait_ge(bonus_ready, t + 1)
                    pe.wait_ge(t1_ready, 2 * LV * t + 2 * l + min(z, 1) + 1)
                    for i, c in enumerate(cs):
                        if l < LV - 1:
                            mm_(bank[4 + z][:, cols(i)], XT[par][:, c, :], T1[:, c, :], start=True, stop=True)
                        mm = mm_(bank[4 + z][:, cols(2 + i)], T1[:, c, :], XT[par][:, c, :], start=True, stop=True)
                    mm.then_inc(xtail_mm if z == 2 else xup_mm, 1)

                def rows_product(c):
                    o1 = bank[0][:, 0:128]
                    o1v = o1.rearrange("p (a t) -> p a t", a=2)
                    if c:
                        pe.wait_ge(y_ready, CHUNKS * j + c)
                    elif later(j):
                        pe.wait_ge(sout_ready, j)
                    if c == 0:
                        pe.wait_ge(stk_ready, j + 1)
                    mm = mm_(o1, TK[m][2][:, c, :], STK[m][:, c, 1:3, :], start=True, stop=True)
                    if c:
                        pe.wait_ge(s_ready, 4 * j + c)
                    if 0 < c < CHUNKS - 1:
                        mm = mm_(o1, SS, AR[m][:, :, C * c:C * c + C], start=False, stop=True, skip_group_check=True)
                    if c == CHUNKS - 1:
                        pe.wait_ge(s0_loaded, 16 * j + 16)
                        mm_(o1v[:, :, 0:TAILP], SS, AR[m][:, :, TAIL:PROMPT], start=False, stop=True, skip_group_check=True)
                        for b in range(NSEQ):
                            a, z = TAILP + TSAMPLE * b, TAILP + TSAMPLE * (b + 1)
                            mm = mm_(o1v[:, :, a:z], S0[:, b, :], AR[m][:, :, TAIL + a:TAIL + z],
                                     start=False, stop=True, skip_group_check=True)
                    mm.then_inc(out1_mm, 1)

                def rhs_transpose(c):
                    pe.wait_ge(rt_ready, CHUNKS * j + c + 1)
                    TRANSPOSE(bank[1][:, 0:128], RT, ident).then_inc(rhs_mm, 1)

                def sa_product(c):
                    pe.wait_ge(rhs_ready, CHUNKS * j + c + 1)
                    mm_(bank[1][:, 128:256], XT[m][:, c, :], RHS, start=True, stop=True).then_inc(sa_mm, 1)

                def state_products(c):
                    pe.wait_ge(sa_ready, CHUNKS * j + c + 1)
                    if c < CHUNKS - 1:
                        mm_(bank[1][:, 256:384], TK[m][0][:, c, :], SA, start=True, stop=False)
                        mm_(bank[1][:, 256:384], TK[m][1][:, c, :], TK[m][2][:, c, :], start=False, stop=True).then_inc(s_mm, 1)
                    mm_(bank[0][:, C:2 * C], SA, STK[m][:, c, 0, :], start=False, stop=True, skip_group_check=True)\
                        .then_inc(y_mm, 1)

                for s_ in range(LV):
                    if inverse:
                        t1_products(s_, 0)
                        if s_ == 0:
                            t1_products(s_, 1)
                    if chain:
                        rows_product(s_)
                    if inverse and s_:
                        t1_products(s_, 1)
                    if operands and s_ == 0:
                        if later(n):
                            pe.wait_ge(gg_ready, n)
                        pe.wait_ge(kksq_ready, n + 1)
                        mm_(bank[7][:, 0:TOK], bones, TB[:, 0:TOK], start=True, stop=True).then_inc(kksum_mm, 1)
                    if operands and s_ == 1:
                        pe.wait_ge(kkroot, n + 1)
                        pe.wait_ge(l2_loaded[m], (8 * n + 16) if m == 0 else (8 * n + 8))
                        mm_(bank[7][:, 0:TOK], L2[m][:, 0:128], hidden[:, 0, :], start=True, stop=True).then_inc(z_mm, 1)
                    if chain:
                        rhs_transpose(s_)
                    if inverse:
                        update_products(s_, 0)
                    if chain:
                        sa_product(s_)
                    if inverse:
                        update_products(s_, 1)
                        if s_ < TAIL_LV:
                            update_products(s_, 2)
                    if operands and s_ == 2:
                        pe.wait_ge(gates_ready, n + 1)
                        mm_(bank[7][:, 0:TOK], L2[m][:, 128:256], hidden[:, 1, :], start=True, stop=True).then_inc(lora_mm, 1)
                    if chain:
                        state_products(s_)
                if operands:
                    pe.wait_ge(bd_ready, n + 1)
                    pe.wait_ge(bdv_ready, n + 1)
                    for i in range(2):
                        for c in range(4):
                            mm = TRANSPOSE(bank[2 + i][:, cols(c)], flat(BD[i], c), ident)
                    mm.then_inc(trans_bk_mm, 1)
                    if inverse:
                        pe.wait_ge(xset_ready[0], LV * t + LV)
                        pe.wait_ge(xset_ready[1], LV * t + LV)
                        pe.wait_ge(xtail_ready, TAIL_LV * t + TAIL_LV)
                    for c in range(4):
                        TRANSPOSE(bank[4][:, cols(c)], flat(BD[2], c), ident)
                    for i in range(3):
                        mm = TRANSPOSE(bank[5][:, cols(i)], flat(BD[i], CHUNKS - 1), ident)
                    mm.then_inc(trans_mm, 1)
                    pe.wait_ge(rkk_ready, n + 1)
                    mm_(bank[6][:, 0:TOK], bones, TB[:, 0:TOK], start=True, stop=True).then_inc(bonus_mm, 1)
                if chain:
                    pe.wait_ge(y_ready, CHUNKS * j + CHUNKS)
                    mm_(bank[7][:, 0:TOK], bones, YY[m], start=True, stop=True).then_inc(mean_mm, 1)
                    pe.wait_ge(sax_ready, j + 1)
                    pe.wait_ge(vx_ready, j + 1)
                    for lo, hi, dst in ((0, 8, bank[1]), (8, 9, bank[0])):
                        mm_(dst[:, 0:C * (hi - lo)], TK[m][0][:, CHUNKS - 1, :], SAX[:, lo:hi, :], start=True, stop=False)
                        mm = mm_(dst[:, 0:C * (hi - lo)], TK[m][1][:, CHUNKS - 1, :], VX[:, lo:hi, :], start=False, stop=True)
                    mm.then_inc(fin_mm, 1)
                if chain:
                    pe.wait_ge(ycsq_ready, j + 1)
                    mm_(bank[7][:, 0:TOK], bones, SQ, start=True, stop=True).then_inc(var_mm, 1)
                if operands:
                    pe.wait_ge(ar_ready, n + 1)
                    pe.wait_ge(tok_act, n + 1)
                    gram = lambda dst, i, c: mm_(dst, flat(BD[i], c), AR[m][:, :, C * c:C * c + C], start=True, stop=True)
                    for c in range(4):
                        gram(bank[2][:, cols(c)], 0, c)
                    for i in range(2):
                        mm = gram(bank[3][:, cols(i)], i, 4)
                    mm.then_inc(gram_b_mm, 1)
                    pe.wait_ge(tok_vec, n + 1)
                    for c in range(4):
                        mm = gram(bank[4][:, cols(c)], 1, c)
                    mm.then_inc(gram_mm, 1)
                if chain:
                    pe.wait_ge(var_ready, j + 1)
                if operands:
                    mm_(bank[7][:, 0:TOK], L2[m][:, 256:384], hidden[:, 2, :], start=True, stop=False)
                    mm_(bank[7][:, 0:TOK], L2[m][:, 384:512], hidden[:, 3, :], start=False, stop=True).then_inc(gate_mm, 1)
                    pe.wait_ge(xt2_ready, n + 1)
                    for c in range(CHUNKS):
                        mm = TRANSPOSE(bank[5][:, cols(c)] if c < 4 else bank[7][:, TOK:TOK + 128], XT[m][:, c, :], ident)
                    mm.then_inc(x2_mm, 1)

            run("v", HHI, HLO, (h_ready, H_BEFORE["mu3"]))
            pe.wait_ge(hid_ready, 4)
            pe.wait_ge(a_free, G["o"] - 2)
            pe.wait_ge(b_free, G["o"] - 2)
            pipeline(iteration, pe.Fori)
            run("o", HHI, HLO, (h_ready, H_BEFORE["o"]))
            mlp(1)
            norm_sum(4)

        @block.scalar
        def _(act):
            steps = Steps(act, act_step)
            activation = nc.scalar.activation

            def split(G_, name, q):
                n = SIZES[name][q] * 128
                act.wait_ge(raw_loaded[q], 16 * G_ + 16)
                act.wait_ge(unit_used, 4 * G_ + (q - 3))
                activation(WHI[q][:, 0:n], RAW[q][:, 0:n], ACT.Copy).then_inc(whi_ready, 1)

            def norm_root(i):
                act.wait_ge(ms_done, i + 1)
                activation(rnorm, meansq, ACT.Sqrt).then_inc(root_done, 1)

            def split_rows(key, src, free, between=None):
                n0 = MADE_BEFORE.get(key)
                if n0 is None:
                    act.wait_ge(out_ready, PAIRS)
                act.wait_ge(unit_used, free)

                def four_tiles(k):
                    for i in range(4):
                        if n0 is not None:
                            act.wait_ge(mix_ready, n0 + 4 * k + (i + 1))
                        activation(HHI[:, 4 * k + i, :], src(4 * k + i, i), ACT.Copy).then_inc(hhi_ready, 1)

                four_tiles(0)
                if between is not None:
                    between()
                with act.Fori(0, KT // 4 - 1) as k:
                    four_tiles(k + 1)

            mixed = lambda k, i: mix[i]

            def up_rows(G_, i, n):
                act.wait_ge(unit_used, 4 * G_ + 2 * i + 2)
                act.wait_ge(conv_ready[i], n + 1)
                act.wait_ge(ulast_saved, 2 * n + 1)
                activation(uext[i][:, 2:2 + PROMPT], prompt(bank[i]), ACT.Copy)
                activation(ext_samples(uext[i], 2)[:, :, 2:], samples(bank[i]), ACT.Copy).then_inc(u_ready, 1)
                act.wait_ge(u_ready, 2 * n + i + 1)
                act.sem_inc((a_free, b_free)[i], 1)
                act.wait_ge(gated, n + 1)
                act.wait_ge(prefix_set[i], n + 1)

            def up(G_, i, n, j):
                col = FT * i + j
                up_rows(G_, i, n)
                activation(conv[i], uext[i][:, 0:CONVW], ACT.Identity, bias=fpar[:, ds(col), 3], scale=fpar[:, ds(col), 0])\
                    .then_inc(c0_ready, 1)
                if i == 1:
                    act.wait_ge(conv_ready[1], n + 2)
                    activation(sgate, conv[1], ACT.Silu).then_inc(silu_ready, 1)
                    act.wait_ge(gated, n + 2)
                    activation(AHI[:, j_local[0], :], act_f, ACT.Copy).then_inc(acthi_ready, 1)

            j_local = [0]

            def evac(name, G_, i, g):
                if name.startswith("in"):
                    layer, s = int(name[2]), int(name[3])
                    j_local[0] = g
                    up(G_, i, FT * layer + SEG0[s] + g, SEG0[s] + g)
                elif name in "krv":
                    act.wait_ge(unit_used, 4 * G_ + 2 * i + 2)
                    dst = {"k": k_all, "r": r_all, "v": v_all}[name]
                    activation(dst[:, 2 * g + i, :], bank[i][:, 0:TOK], ACT.Copy).then_inc((a_free, b_free)[i], 1)
                elif name == "lora":
                    act.wait_ge(unit_used, 4 * G_ + 2 * i + 2)
                    n = 2 * g + i
                    if n == 0:
                        activation(hidden[:, 0, :], bank[i][:, 0:TOK], ACT.Tanh).then_inc(a_free, 1)
                    elif n == 1:
                        activation(hidden[:, 1, :], bank[i][:, 0:TOK], ACT.Copy).then_inc(b_free, 1)
                    else:
                        activation(hidden[:, n, :], bank[i][:, 0:TOK], ACT.Tanh, scale=0.5).then_inc((a_free, b_free)[i], 1)

            def iteration(t, par_, operands=True, inverse=True, chain=True, finish=True):
                n, m, j = t + 1, 1 - par_, t - 1
                if operands:
                    if later(n):
                        act.wait_ge(bonus_mm, n)
                    activation(TB[:, 0:TOK], k_all[:, n, :], ACT.Square, scale=par("kk", n)).then_inc(kksq_ready, 1)
                for s_ in range(LV):
                    c = CHUNKS * j + s_

                    def x_evac(b, cs, ready):
                        k = len(cs)
                        dst = lambda X: X[:, cs[0]:cs[0] + k, :]
                        src = lambda o: bank[b][:, o:o + 128 * k].rearrange("p (c n) -> p c n", c=k)
                        if s_ < LV - 1:
                            activation(dst(XM), src(0), ACT.Copy)
                        activation(dst(XT[par_]), src(256), ACT.Copy).then_inc(ready, 1)

                    if chain:
                        if 0 < s_ < CHUNKS - 1:
                            act.wait_ge(s_ready, 4 * j + s_)
                            activation(SP, SS, ACT.Copy, scale=PP[m][:, C * s_ + C - 1:C * s_ + C]).then_inc(sp_ready, 1)
                        act.wait_ge(rhs_mm, c + 1)
                        activation(RHS, bank[1][:, 0:128], ACT.Copy).then_inc(rhs_ready, 1)
                    if inverse:
                        act.wait_ge(xup_mm, 2 * LV * t + 2 * s_ + 1)
                        x_evac(4, (0, 1), xset_ready[0])
                    if chain:
                        act.wait_ge(sa_mm, c + 1)
                        activation(SA, bank[1][:, 128:256], ACT.Copy).then_inc(sa_ready, 1)
                    if inverse and s_ < TAIL_LV:
                        act.wait_ge(xtail_mm, TAIL_LV * t + s_ + 1)
                        x_evac(6, (CHUNKS - 1,), xtail_ready)
                    if chain:
                        act.wait_ge(y_mm, c + 1)
                        w = min(C, TOK - C * s_)
                        activation(YY[m][:, C * s_:C * s_ + w], bank[0][:, C:C + w], ACT.Copy).then_inc(y_ready, 1)
                    if inverse and s_ == 0:
                        act.wait_ge(ar_ready, t + 1)
                        if chain and later(j):
                            act.wait_ge(fin_ready, j)
                        activation(PP[par_], PPT[:, 0:TOK], ACT.Copy).then_inc(pend_ready, 1)
                    if finish and s_ == 0:
                        act.wait_ge(scaled, t - 1)
                        activation(YY[par_], YY[par_], ACT.Identity, scale=par("lnw", t - 2), bias=par("lnb", t - 2)).then_inc(affine, 1)
                    if finish and s_ == 1:
                        act.wait_ge(out_ready, t - 1)
                    if operands and s_ == 0:
                        act.wait_ge(kksum_mm, n + 1)
                        activation(TC[:, 0:TOK], bank[7][:, 0:TOK], ACT.Sqrt).then_inc(kkroot, 1)
                    if operands and s_ == 1:
                        act.wait_ge(z_mm, n + 1)
                        steps.done(activation(DEC[:, 0:TOK], bank[7][:, 0:TOK], ACT.Tanh, bias=w0_half[:, ds(n)], scale=0.5))
                        steps.wait()
                        activation(DEC[:, 0:TOK], DEC[:, 0:TOK], ACT.Exp, scale=0.5 * DECAY_SCALE, bias=decay_bias)\
                            .then_inc(gates_ready, 1)
                    if operands and s_ == 2:
                        act.wait_ge(lora_mm, n + 1)
                        steps.done(activation(TA[:, 0:TOK], bank[7][:, 0:TOK], ACT.Tanh, bias=a0_half[:, ds(n)], scale=0.5))
                        steps.wait()
                        activation(KP[:, 0:TOK], TA[:, 0:TOK], ACT.Identity, scale=ka_half[:, ds(n)], bias=ka_rest[:, ds(n)])\
                            .then_inc(kp_ready, 1)
                if operands:
                    act.wait_ge(trans_bk_mm, n + 1)
                    activation(TK[m][0][:, 0:4, :], bank[2].rearrange("p (c n) -> p c n", c=4), ACT.Copy)
                    activation(TK[m][1][:, 0:4, :], bank[3].rearrange("p (c n) -> p c n", c=4), ACT.Copy).then_inc(tok_act, 1)
                if chain:
                    act.wait_ge(centered, j + 1)
                    activation(SQ, YY[m], ACT.Square).then_inc(ycsq_ready, 1)
                    act.wait_ge(var_ready, j + 1)
                    activation(SD, SD, ACT.Sqrt).then_inc(gnroot, 1)
                if operands:
                    act.wait_ge(gate_mm, n + 1)
                    act.wait_ge(x2_mm, n + 1)
                    for z in range(2):
                        ins = activation(XM[:, 2 * z:2 * z + 2, :], bank[5][:, 256 * z:256 * z + 256]
                                         .rearrange("p (c n) -> p c n", c=2), ACT.Copy)
                        if z == 0:
                            ins.then_inc(x2_ready, 1)
                    activation(XM[:, 4, :], bank[7][:, TOK:TOK + 128], ACT.Copy).then_inc(x2_ready, 1)
                    activation(k_all[:, n, :], bank[7][:, 0:TOK], ACT.Copy).then_inc(gg_ready, 1)

            decay_bias = 0.5 * DECAY_SCALE

            def square(k):
                activation(mix[k % 4], x[:, k, :], ACT.Square).then_inc(squared, 1)

            def square_pooled(k):
                act.wait_ge(x_done, k + 1)
                if k >= 4:
                    act.wait_ge(sq_done, k - 3)
                square(k)

            for k in range(KT):
                act.wait_ge(x_loaded[k // 4], 16)
                if k >= 4:
                    act.wait_ge(sq_used, k - 3)
                square(k)
            act.wait_ge(in_loaded, 32)
            norm_root(0)
            act.sem_inc(whi_ready, end("pool"))
            act.wait_ge(sq_used, KT)
            for k in range(8):
                square_pooled(k)
            for q in range(4):
                split(G["in00"], "in00", q)
                square_pooled(8 + 2 * q)
                square_pooled(9 + 2 * q)

            prev = None

            def transition(name):
                if name == "in00":
                    norm_root(1)
                    act.wait_ge(pool_evac, 16)
                    split_rows("ffn0", mixed, end("pool"))
                elif name == "in10":
                    norm_root(3)
                    split_rows("ffn1", mixed, end("o"))
                elif name in "krv":
                    split_rows(MIXES[name], mixed, {"k": end("lora"), "r": end("k"), "v": end("r")}[name],
                               lambda: split(G[name], name, 3))
                elif name == "o":
                    act.wait_ge(chunk_clear, 1)
                    pipeline(iteration, act.Fori, steps, 2)
                    split_rows("o", lambda k, i: r_all[:, k, :], end("v"))

            for name in NAMES[1:]:
                g0, n = G[name], COUNT[name]
                if prev:
                    split(g0, name, 0)
                    split(g0, name, 1)
                    evac(prev, g0 - 1, 0, COUNT[prev] - 1)
                    split(g0, name, 2)
                    evac(prev, g0 - 1, 1, COUNT[prev] - 1)
                    if name not in "krv":
                        split(g0, name, 3)
                if name == "lora":
                    norm_root(2)
                    split_rows("mu1", mixed, end("out02"))
                    split_rows("mu4", mixed, 4 * g0 + 2, lambda: (split(g0 + 1, "lora", 0), split(g0 + 1, "lora", 1)))
                    evac("lora", g0, 0, 0)
                    split(g0 + 1, name, 2)
                    evac("lora", g0, 1, 0)
                    split_rows("mu5", mixed, 4 * g0 + 4, lambda: split(g0 + 1, "lora", 3))
                else:
                    transition(name)
                    if n > 1:
                        with act.Fori(0, n - 1) as g:
                            for q in range(4):
                                split(g0 + 1 + g, name, q)
                                if q % 2:
                                    evac(name, g0 + g, q // 2, g)
                prev = name
            norm_root(4)

        @block.vector
        def _(vec):
            steps = Steps(vec, vec_step)
            tt, ts, stt = nc.vector.tensor_tensor, nc.vector.tensor_scalar, nc.vector.scalar_tensor_tensor

            def link(ins):
                steps.done(ins)
                steps.wait()

            def split(G_, name, q):
                n = SIZES[name][q] * 128
                vec.wait_ge(whi_ready, 4 * G_ + q + 1)
                tt(WLO[q][:, 0:n], RAW[q][:, 0:n], WHI[q][:, 0:n].bitcast(f32), ALU.subtract).then_inc(wlo_ready, 1)

            def norm_scale(i):
                vec.wait_ge(*((sq_used, KT) if i == 0 else (sums_done, i)))
                ts(meansq, bank[7][:, 0:TOK], 1.0 / D, NORM_EPS, ALU.mult, ALU.add).then_inc(ms_done, 1)
                vec.wait_ge(root_done, i + 1)
                link(nc.vector.reciprocal(rnorm, rnorm))

            def rest_rows(key, make, src, between=None):
                n0 = H_BEFORE[key]

                def two_tiles(k, i):
                    if make is not None:
                        for d in (2, 3):
                            if later(k) or i:
                                vec.wait_ge(h_ready, n0 + 4 * k + (i + d - 3))
                            make(4 * k + i + d, (i + d) % 4).then_inc(mix_ready, 1)
                    rests(k, i)

                def rests(k, i):
                    for d in (0, 1):
                        vec.wait_ge(hhi_ready, n0 + 4 * k + (i + d + 1))
                        tt(HLO[:, 4 * k + i + d, :], src(4 * k + i + d, i + d), HHI[:, 4 * k + i + d, :].bitcast(f32), ALU.subtract)\
                            .then_inc(h_ready, 1)

                if make is not None:
                    for i in range(2):
                        make(i, i).then_inc(mix_ready, 1)
                two_tiles(0, 0)
                two_tiles(0, 2)
                if between is not None:
                    between()
                with vec.Fori(0, KT // 4 - 2) as g:
                    two_tiles(1 + g, 0)
                    two_tiles(1 + g, 2)
                two_tiles(KT // 4 - 1, 0)
                rests(KT // 4 - 1, 2)
                vec.wait_ge(h_ready, n0 + KT)

            mixed = lambda k, i: mix[i]

            def mix_rows(m, between=None):
                mu = MIXES[m]
                rest_rows(mu, lambda k, i: stt(mix[i], xx[:, k, :], par(mu, k), h[:, k, :], ALU.mult, ALU.add), mixed,
                          (lambda: split(G[m], m, 3)) if m in "krv" else between)

            def evac(name, G_, i, g):
                if name.startswith("in"):
                    layer, s = int(name[2]), int(name[3])
                    n, j = FT * layer + SEG0[s] + g, SEG0[s] + g
                    col = FT * i + j
                    vec.wait_ge(c0_ready, 2 * n + i + 1)
                    for tap in (1, 2):
                        ins = stt(conv[i], uext[i][:, tap:tap + CONVW], fpar[:, ds(col), tap], conv[i], ALU.mult, ALU.add)
                        if tap == 1:
                            link(ins)
                    ins.then_inc(conv_ready[i], 1)
                    if i == 1:
                        vec.wait_ge(silu_ready, n + 1)
                        vec.wait_ge(conv_ready[0], n + 2)
                        tt(act_f[:, 0:PROMPT], conv[0][:, 0:PROMPT], sgate[:, 0:PROMPT], ALU.mult)
                        tt(samples(act_f), ext_tail(conv[0]), ext_tail(sgate), ALU.mult).then_inc(gated, 1)
                        vec.wait_ge(acthi_ready, n + 1)
                        tt(ALO[:, g, :], act_f, AHI[:, g, :].bitcast(f32), ALU.subtract).then_inc(act_ready, 1)
                elif name.startswith("out") or name == "o":
                    vec.wait_ge(unit_used, 4 * G_ + 2 * i + 2)
                    m = 2 * g + i
                    tt(x[:, m, :], bank[i][:, 0:TOK], x[:, m, :], ALU.add).then_inc(x_done, 1)
                    vec.wait_ge(x_done, OUT_X[name] + m + 1)
                    vec.sem_inc((a_free, b_free)[i], 1)

            def ext_tail(t):
                return t[:, PROMPT:].rearrange("p (b e) -> p b e", b=NSEQ)[:, :, 2:]

            def iteration(t, par_, operands=True, inverse=True, chain=True, finish=True):
                n, m, j = t + 1, 1 - par_, t - 1
                T = slice(0, TOK)
                copy = nc.vector.tensor_copy
                starts = lambda a: (a[:, 0:PROMPT:C], a[:, PROMPT:TOK:TSAMPLE])
                halves = (slice(0, 64), slice(64, 128))
                chunked = lambda a, r: a[r, :].rearrange("p (c t) -> p c t", c=CHUNKS)
                lev = lambda l, k: con("lev")[:, 128 * l:128 * l + 128].rearrange("p (o w) -> p o w", o=1).broadcast_to([128, k, 128])

                def decays():
                    vec.wait_ge(gates_ready, n + 1)
                    for z, d in zip(starts(ZD), starts(DEC)):
                        ins = copy(z, d)
                    link(ins)
                    for d in starts(DEC):
                        ins = nc.vector.memset(d, 0.0)
                    link(ins)
                    if later(n):
                        vec.wait_ge(pend_ready, n)
                    link(nc.vector.tensor_tensor_scan(PPT[:, T], DEC[:, T], ZD, 0.0, ALU.mult, ALU.add))

                    nc.vector.reciprocal(PIN[:, T], PPT[:, T])

                def norms():
                    vec.wait_ge(kkroot, n + 1)
                    link(ts(TC[:, T], TC[:, T], 1e-12, None, ALU.max))
                    link(nc.vector.reciprocal(TC[:, T], TC[:, T]))
                    stt(NKK[:, T], k_all[:, n, :], kk_neg[:, ds(n)], TC[:, T], ALU.mult, ALU.mult)

                def b_rows():
                    vec.wait_ge(kp_ready, n + 1)
                    tt(KP[:, T], KP[:, T], k_all[:, n, :], ALU.mult)
                    link(stt(TA[:, T], TA[:, T], 1.0, NKK[:, T], ALU.add, ALU.mult))
                    for a, r in enumerate(halves):
                        stt(BD[0][r, :, a, :], chunked(TA, r), -0.5, chunked(PIN, r), ALU.mult, ALU.mult)

                def k_rows():
                    for a, r in enumerate(halves):
                        ins = tt(BD[1][r, :, a, :], chunked(KP, r), chunked(PIN, r), ALU.mult)
                    ins.then_inc(bd_ready, 1)
                    stt(TB[:, T], r_all[:, n, :], par("rk", n), KP[:, T], ALU.mult, ALU.mult).then_inc(rkk_ready, 1)

                steps_n = {1: norms, 2: decays, 3: b_rows, 4: k_rows}
                for s_ in range(LV):
                    tail = s_ < TAIL_LV

                    def t1(z):
                        vec.wait_ge(t1_mm, 2 * LV * t + 2 * s_ + z + 1)
                        k = 3 if z and tail else 2
                        tt(T1[:, 2 * z:2 * z + k, :], bank[2 + z][:, 0:128 * k].rearrange("p (c n) -> p c n", c=k),
                           lev(s_ + 1, k), ALU.mult).then_inc(t1_ready, 1)

                    if inverse:
                        t1(0)
                        if s_ == 0:
                            t1(1)
                    if chain:
                        vec.wait_ge(out1_mm, CHUNKS * j + s_ + 1)
                        tt(RT.rearrange("p (a t) -> p a t", a=2),
                           bank[0][:, 0:C].rearrange("p (o t) -> p o t", o=1).broadcast_to([128, 2, C]),
                           half.rearrange("p (a o) -> p a o", o=1).broadcast_to([128, 2, C]), ALU.mult).then_inc(rt_ready, 1)
                    if inverse and s_:
                        t1(1)
                    if inverse and s_ == 0:
                        vec.wait_ge(bonus_mm, t + 1)
                        tt(r_all[:, t, :], bank[6][:, T], v_all[:, t, :], ALU.mult).then_inc(bonus_ready, 1)
                    if finish and s_ == 0:
                        vec.wait_ge(gnroot, t - 1)
                        link(nc.vector.reciprocal(SD, SD))
                        tt(YY[par_], YY[par_], SD, ALU.mult).then_inc(scaled, 1)
                    if operands and s_ in steps_n:
                        steps_n[s_]()
                    if inverse:
                        vec.wait_ge(xup_mm, 2 * LV * t + 2 * s_ + 2)
                        two = lambda o: bank[5][:, o:o + 256].rearrange("p (c n) -> p c n", c=2)
                        if s_ < LV - 1:
                            copy(XM[:, 2:4, :], two(0))
                        copy(XT[par_][:, 2:4, :], two(256)).then_inc(xset_ready[1], 1)
                    if chain and s_ < CHUNKS - 1:
                        vec.wait_ge(s_mm, 4 * j + s_ + 1)
                        pend = PP[m][:, C * s_ + C - 1:C * s_ + C]
                        if s_ == 0:
                            ts(SS, bank[1][:, 256:384], pend, None, ALU.mult).then_inc(s_ready, 1)
                        else:
                            vec.wait_ge(sp_ready, 3 * j + s_)
                            stt(SS, bank[1][:, 256:384], pend, SP, ALU.mult, ALU.add).then_inc(s_ready, 1)
                if operands:
                    tt(AR[m][:, 0, 1:TOK], NKK[:, 1:TOK], PPT[:, 0:TOK - 1], ALU.mult)
                    link(tt(AR[m][:, 1, T], r_all[:, n, :], PPT[:, T], ALU.mult))
                    for z, d in zip(starts(AR[m][:, 0, :]), starts(NKK)):
                        ins = copy(z, d)
                    ins.then_inc(ar_ready, 1)
                if operands:
                    vec.wait_ge(trans_mm, n + 1)
                    copy(TK[m][2][:, 0:4, :], bank[4].rearrange("p (c n) -> p c n", c=4))
                if chain:
                    vec.wait_ge(mean_mm, j + 1)
                    stt(YY[m], bank[7][:, T], -1.0 / HS, YY[m], ALU.mult, ALU.add).then_inc(centered, 1)
                if chain:
                    vec.wait_ge(fin_mm, j + 1)
                if operands:
                    for i in range(3):
                        ins = copy(TK[m][i][:, 4, :], bank[5][:, 128 * i:128 * i + 128])
                    ins.then_inc(tok_vec, 1)
                if chain:
                    vec.wait_ge(var_mm, j + 1)
                    ts(SD, bank[7][:, T], 1.0 / HS, GN_EPS, ALU.mult, ALU.add).then_inc(var_ready, 1)
                if operands:
                    def mask(name, k, w0, w1):
                        w = w1 - w0
                        return con(name).rearrange("p (o w t) -> p o w t", o=1, t=C)[:, :, w0:w1, :].broadcast_to([128, k, w, C])
                    gb = bank[2].rearrange("p (c w t) -> p c w t", c=4, w=2)
                    gk = bank[4].rearrange("p (c w t) -> p c w t", c=4, w=2)
                    g4 = bank[3][:, 0:256].rearrange("p (c w t) -> p c w t", c=1, w=4)
                    ltv = LT.rearrange("p c (a t) -> p c a t", a=2)
                    vec.wait_ge(gram_b_mm, n + 1)
                    tt(ltv[:, 0:4, :, :], gb[:, :, 0:1, :].broadcast_to([128, 4, 2, C]), mask("lt", 4, 0, 2), ALU.mult)
                    link(tt(ltv[:, 4:5, :, :], g4[:, :, 0:1, :].broadcast_to([128, 1, 2, C]), mask("lt_tail", 1, 0, 2), ALU.mult))
                    link(tt(LT, LT, ident.rearrange("p (o w) -> p o w", o=1).broadcast_to([128, CHUNKS, 128]), ALU.add))
                    tt(XT[m], LT, lev(0, CHUNKS), ALU.mult).then_inc(xt2_ready, 1)
                    tt(STK[m][:, 0:4, 0:1, :], gb[:, :, 1:2, :], mask("stk", 4, 0, 1), ALU.mult)
                    tt(STK[m][:, 4:5, :, :], g4[:, :, 1:4, :], mask("stk_tail", 1, 0, 3), ALU.mult).then_inc(grams_left, 1)
                    vec.wait_ge(gram_mm, n + 1)
                    tt(STK[m][:, 0:4, 1:3, :], gk, mask("stk", 4, 1, 3), ALU.mult).then_inc(stk_ready, 1)
                if chain:
                    for r in halves:
                        tt(SOUT[r, 0:8, :], bank[1][r, :].rearrange("p (b v) -> p b v", b=NSEQ), S0[r, :, r], ALU.add)
                        ins = tt(SOUT[r, 8, :], bank[0][r, 0:C], SS[r, r], ALU.add)
                    ins.then_inc(sout_ready, 1)

            for s_ in (*conv_ready, gated):
                vec.sem_inc(s_, 1)
            nc.vector.memset(ones, 1.0).then_inc(ones_set, 1)
            vec.wait_ge(in_loaded, 32)
            ts(w0_half, PAR[:, PCOL["w0"]:PCOL["w0"] + KT], 0.5, None, ALU.mult)
            ts(a0_half, PAR[:, PCOL["a0"]:PCOL["a0"] + KT], 0.5, None, ALU.mult)
            ts(ka_half, PAR[:, PCOL["ka"]:PCOL["ka"] + KT], 0.5, None, ALU.mult)
            ts(ka_rest, PAR[:, PCOL["ka"]:PCOL["ka"] + KT], -0.5, 1.0, ALU.mult, ALU.add)
            link(ts(kk_neg, PAR[:, PCOL["kk"]:PCOL["kk"] + KT], -1.0, None, ALU.mult))
            vec.sem_inc(wlo_ready, end("pool"))
            norm_scale(0)
            vec.wait_ge(pst_loaded, 32)
            vec.wait_ge(pool_clear, 1)

            def pooled_x(g, q):
                vec.wait_ge(unit_used, 4 * g + q + 1)
                for i in range(2):
                    m = 8 * g + 2 * q + i
                    stt(x[:, m, :], bank[2 * q + i][:, 0:TOK], par("scale", m), x[:, m, :], ALU.mult, ALU.add)\
                        .then_inc(pool_evac, 1)
                    vec.wait_ge(pool_evac, m + 1)
                    vec.sem_inc(x_done, 1)

            for grp in (3, 2, 0, 1):
                for k in range(4 * grp, 4 * grp + 4):
                    stt(pext[:, k, POOL_STATE:POOL_STATE + PROMPT], prompt(x[:, k, :]), par("mix0", k), prompt(rnorm), ALU.mult, ALU.mult)
                    ins = stt(ext_samples(pext[:, k, :], POOL_STATE)[:, :, POOL_STATE:], samples(x[:, k, :]),
                              par("mix0", k), samples(rnorm), ALU.mult, ALU.mult)
                ins.then_inc(pooled_norm, 1)
            vec.wait_ge(pooled_norm, 4)
            for grp in range(4):
                if grp < 2:
                    src = windows(tt, grp, win, link)
                else:
                    vec.wait_ge(win_ready, 4 - grp)
                    src = win[4] if grp == 3 else win[3]
                hh = pext[:, 4 * grp:4 * grp + 4, :]
                rc = rcnt[:, grp:grp + 1, :].broadcast_to([128, 4, TOK])
                pdiff = pdiff_all[:, 4 * grp:4 * grp + 4, :]
                tt(pdiff[:, :, 0:PROMPT], src[:, :, POOL_STATE:POOL_STATE + PROMPT], rc[:, :, 0:PROMPT], ALU.mult)
                for k in range(4):
                    ins = ts(samples(pdiff[:, k, :]), ext_samples(src[:, k, :], POOL_STATE)[:, :, POOL_STATE:],
                             1.0 / WINDOWS[grp], None, ALU.mult)
                link(ins)
                tt(pdiff[:, :, 0:PROMPT], pdiff[:, :, 0:PROMPT], hh[:, :, POOL_STATE:POOL_STATE + PROMPT], ALU.subtract)
                for k in range(4):
                    ins = tt(samples(pdiff[:, k, :]), samples(pdiff[:, k, :]),
                             ext_samples(hh[:, k, :], POOL_STATE)[:, :, POOL_STATE:], ALU.subtract)
                ins.then_inc(pdiff_ready, 1)
                if grp in (1, 2):
                    pooled_x(0, 2 * grp - 2)
                    pooled_x(0, 2 * grp - 1)
            for q in range(4):
                pooled_x(1, q)
                split(G["in00"], "in00", q)

            def normed(name):
                return lambda k, i: stt(mix[i], x[:, k, :], par(name, k), rnorm, ALU.mult, ALU.mult)

            prev = None
            for name in NAMES[1:]:
                g0, n = G[name], COUNT[name]
                if prev:
                    split(g0, name, 0)
                    split(g0, name, 1)
                    evac(prev, g0 - 1, 0, COUNT[prev] - 1)
                    split(g0, name, 2)
                    evac(prev, g0 - 1, 1, COUNT[prev] - 1)
                    if name not in "krv":
                        split(g0, name, 3)
                if name == "in00":
                    norm_scale(1)
                    rest_rows("ffn0", normed("ffn0"), mixed)
                    vec.wait_ge(pool_stored, 16)
                elif name == "in10":
                    norm_scale(3)
                    rest_rows("ffn1", normed("ffn1"), mixed)
                elif name == "lora":
                    norm_scale(2)
                    vec.wait_ge(conv0_stored, 16)
                    vec.wait_ge(shift_loaded, 16)
                    with vec.Fori(0, KT // 4) as k:
                        for i in range(4):
                            stt(h[:, 4 * k + i, :], x[:, 4 * k + i, :], par("mix1", 4 * k + i), rnorm, ALU.mult, ALU.mult)\
                                .then_inc(h0_ready, 1)
                    vec.wait_ge(h0_ready, KT)
                    nc.vector.tensor_copy(shlast[:, :, 0:1], h[:, :, PROMPT - 1:PROMPT])
                    nc.vector.tensor_copy(shlast[:, :, 1:9], h[:, :, PROMPT + TSAMPLE - 1:TOK:TSAMPLE]).then_inc(shlast_ready, 1)
                    shifted(tt, ts, link, 0, XX_SPLIT)
                    mix_rows("w", lambda: vec.wait_ge(xx_ready, 1))
                    mix_rows("a", lambda: (split(g0 + 1, "lora", 0), split(g0 + 1, "lora", 1)))
                    split(g0 + 1, name, 2)
                    mix_rows("g", lambda: split(g0 + 1, "lora", 3))
                elif name == "k":
                    vec.wait_ge(b_free, G["k"] - 2)
                    vec.wait_ge(a_free, G["k"] - 2)
                    ts(hidden[:, 2:4, :], hidden[:, 2:4, :], 0.5, 0.5, ALU.mult, ALU.add).then_inc(hid_ready, 4)
                    mix_rows("k")
                elif name == "r":
                    mix_rows("r")
                elif name == "v":
                    mix_rows("v")
                elif name == "o":
                    vec.wait_ge(chunk_clear, 1)
                    pipeline(iteration, vec.Fori, steps, RSTEPS)
                    rest_rows("o", None, lambda k, i: r_all[:, k, :])
                    vec.wait_ge(refilled, 16)
                if name != "lora":
                    per = 2 if name.startswith("in") else 0
                    if n > 1:
                        with vec.Fori(0, n - 1) as g:
                            steps.enter(g, per)
                            for q in range(4):
                                split(g0 + 1 + g, name, q)
                                if q % 2:
                                    evac(name, g0 + g, q // 2, g)
                        steps.leave(n - 1)
                prev = name
            for i in range(2):
                evac(prev, GROUPS - 1, i, COUNT[prev] - 1)
            norm_scale(4)
            with vec.Fori(0, KT // 4) as k:
                for i in range(4):
                    stt(x[:, 4 * k + i, :], x[:, 4 * k + i, :], par("out", 4 * k + i), rnorm, ALU.mult, ALU.mult).then_inc(out_tile, 1)

        @block.gpsimd
        def _(pool):
            steps = Steps(pool, pool_step)

            def square_sums(i):
                if i > 1:
                    pool.wait_ge(sums_done, i - 1)
                steps.done(nc.gpsimd.memset(sumsq, 0.0))
                with pool.Fori(0, KT) as k:
                    steps.enter(k, 2)
                    pool.wait_ge(x_done, X_BEFORE[i] - KT + k + 1)
                    steps.wait()
                    steps.done(nc.gpsimd.tensor_tensor(squares, x[:, k, :], x[:, k, :], ALU.mult))
                    steps.wait()
                    steps.done(nc.gpsimd.tensor_tensor(sumsq, sumsq, squares, ALU.add))
                    steps.wait()
                    pool.sem_inc(sq_done, 1)
                steps.leave(KT)

            def mlp_rows(layer):
                if layer == 0:
                    pool.wait_ge(pool_stored, 16)
                pool.wait_ge(ffn_loaded, 32 * (layer + 1))
                for i in range(2):
                    ins = nc.gpsimd.memset(uext[i][:, 0:2], 0.0)
                steps.done(ins)
                steps.wait()
                with pool.Fori(0, FT) as j:
                    n = FT * layer + j
                    for i in range(2):
                        col = FT * i + j
                        pool.wait_ge(conv_ready[i], n + 1)
                        nc.gpsimd.tensor_copy(ext_samples(uext[i], 2)[:, :, 0:2],
                                              prefix[:, ds(col), :].rearrange("p o (b e) -> p (o b) e", b=NSEQ)).then_inc(prefix_set[i], 1)
                        pool.wait_ge(u_ready, 2 * n + i + 1)
                        nc.gpsimd.tensor_copy(ulast[:, ds(col), 0:2], uext[i][:, PROMPT:PROMPT + 2].rearrange("p (o b) -> p o b", o=1))
                        nc.gpsimd.tensor_copy(ulast[:, ds(col), 2:18].rearrange("p o (b e) -> p (o b) e", b=NSEQ),
                                              ext_samples(uext[i], 2)[:, :, 4:6]).then_inc(ulast_saved, 1)

            pool.sem_inc(ulast_saved, 1)
            pool.wait_ge(in_loaded, 32)
            steps.done(nc.gpsimd.memset(pext[:, :, 0:POOL_STATE], 0.0))
            steps.wait()
            pool.sem_inc(pool_clear, 1)
            def pool_link(ins):
                steps.done(ins)
                steps.wait()

            for grp in (3, 2):
                pool.wait_ge(pooled_norm, 4 - grp)
                windows(nc.gpsimd.tensor_tensor, grp, (win[2], win[4]) if grp == 3 else (win[3], win[2]), pool_link)
                pool.sem_inc(win_ready, 1)
            steps.done(nc.gpsimd.memset(sumsq, 0.0))
            steps.wait()
            for k in range(KT):
                pool.wait_ge(squared, KT + k + 1)
                steps.done(nc.gpsimd.tensor_tensor(sumsq, sumsq, mix[k % 4], ALU.add))
                steps.wait()
                pool.sem_inc(sq_done, 1)
            mlp_rows(0)
            square_sums(2)
            pool.wait_ge(h0_ready, KT)
            pool.wait_ge(shift_loaded, 16)
            shifted(nc.gpsimd.tensor_tensor, nc.gpsimd.tensor_scalar, pool_link, XX_SPLIT, KT)
            pool.sem_inc(xx_ready, 1)
            pool.wait_ge(h_ready, H_BEFORE["o"])
            pool.wait_ge(spilled, 16)
            pool.wait_ge(shift_stored, 16)
            for t in (*BD, ZD, *[b[:, TOK:] for b in (TA, PIN, KP)]):
                nc.gpsimd.memset(t, 0.0)
            pool.wait_ge(unit_used, end("v"))
            for b in AR:
                ins = nc.gpsimd.memset(b[:, :, TOK:], 0.0)
            steps.done(ins)
            steps.wait()
            pool.sem_inc(chunk_clear, 1)
            pool.wait_ge(b_free, G["o"] - 2)

            def copies(dst, src, r):
                return nc.gpsimd.tensor_tensor(
                    dst[r, :, :], src[r, r].rearrange("p (o v) -> p o v", o=1).broadcast_to([64, 9, C]),
                    con("seq")[r, :].rearrange("p (s o) -> p s o", o=1).broadcast_to([64, 9, C]), ALU.mult)

            def iteration(t, par_, operands=True, inverse=True, chain=True, finish=True):
                n, m, j = t + 1, 1 - par_, t - 1
                halves = (slice(0, 64), slice(64, 128))
                if operands:
                    if later(n):
                        pool.wait_ge(trans_mm, n)
                    for a, r in enumerate(halves):
                        nc.gpsimd.tensor_copy(BD[2][r, 0:4, a, :], v_all[r, n, 0:TAIL].rearrange("p (c t) -> p c t", c=4))
                        ins = nc.gpsimd.tensor_copy(BD[2][r, 4, a, 0:TOK - TAIL], v_all[r, n, TAIL:TOK])
                    ins.then_inc(bdv_ready, 1)
                    pool.wait_ge(bdv_ready, n + 1)
                if finish:
                    pool.wait_ge(affine, t - 1)
                    steps.done(nc.gpsimd.tensor_tensor(YY[par_], YY[par_], r_all[:, t - 2, :], ALU.add))
                    steps.wait()
                    nc.gpsimd.tensor_tensor(r_all[:, t - 2, :], YY[par_], k_all[:, t - 2, :], ALU.mult).then_inc(out_ready, 1)
                    pool.wait_ge(out_ready, t - 1)
                if chain:
                    pool.wait_ge(sa_ready, CHUNKS * j + CHUNKS)
                    for r in halves:
                        ins = copies(SAX, SA, r)
                    ins.then_inc(sax_ready, 1)
                    pool.wait_ge(sax_ready, j + 1)
                if inverse:
                    pool.wait_ge(tok_vec, t + 1)
                    if chain:
                        pool.wait_ge(fin_mm, t)
                    for r in halves:
                        ins = copies(VX, TK[par_][2][:, CHUNKS - 1, :], r)
                    ins.then_inc(vx_ready, 1)
                    pool.wait_ge(vx_ready, t + 1)
                if chain:
                    pool.wait_ge(sout_ready, j + 1)
                    nc.gpsimd.tensor_tensor(
                        SOUT[:, 0:8, :], SOUT[:, 0:8, :], PP[m][:, PROMPT + TSAMPLE - 1:TOK:TSAMPLE]
                        .rearrange("p (b o) -> p b o", o=1).broadcast_to([128, NSEQ, C]), ALU.mult)
                    nc.gpsimd.tensor_scalar(SOUT[:, 8, :], SOUT[:, 8, :], PP[m][:, PROMPT - 1:PROMPT], None, ALU.mult).then_inc(fin_ready, 1)
                    pool.wait_ge(fin_ready, j + 1)

            pipeline(iteration, pool.Fori, steps, 1)
            square_sums(3)
            mlp_rows(1)
            square_sums(4)


def lay_out(v):
    f = {n: np.asarray(a) for n, a in v.items()}

    def feat(a):
        a = np.moveaxis(a, -1, 0)
        return np.ascontiguousarray(np.moveaxis(a.reshape(KT, 128, *a.shape[1:]), 0, 1))

    def columns(w):
        k, m = w.shape
        return w.reshape(k // 128, 128, m // 128, 128).transpose(2, 1, 0, 3)

    def widened(w):
        return np.concatenate([w, np.zeros((w.shape[0], 128 - w.shape[1]), w.dtype)], 1)

    units = np.zeros((4 * GROUPS, 128, 8, 128), np.float32)

    def place(name, cols):
        u = 4 * FIRST[name]
        k = cols.shape[2]
        n = cols.shape[0]
        units[u:u + 2 * n:2] = cols[:, :, 0:8]
        units[u + 1:u + 2 * n:2, :, 0:k - 8] = cols[:, :, 8:]

    pw = f["pool_w"][0]
    for grp in range(4):
        c = columns(pw[grp])
        units[2 * grp:2 * grp + 2] = c.reshape(2, 2, 128, 4, 128).transpose(0, 2, 1, 3, 4).reshape(2, 128, 8, 128)
    for l in range(LAYERS):
        cin, cout = columns(f["ffn_w_in"][l]), columns(f["ffn_w_out"][l])
        for s, n in enumerate(SEGS):
            a = SEG0[s]
            both = np.stack([cin[a:a + n], cin[FT + a:FT + a + n]], 1).reshape(2 * n, 128, KT, 128)
            place(f"in{l}{s}", both)
            place(f"out{l}{s}", cout[:, :, a:a + n])
    place("lora", columns(np.concatenate([widened(f["rwkv_w1"][0]), widened(f["rwkv_a1"][0]), f["rwkv_g1"][0]], 1)))
    for name, w in (("k", "rwkv_wk"), ("r", "rwkv_wr"), ("v", "rwkv_wv"), ("o", "rwkv_wo")):
        place(name, columns(f[w][0]))
    l2 = np.zeros((PAIRS, 128, 4, 128), np.float32)
    l2[:, 0:LORA, 0] = f["rwkv_w2"][0].reshape(LORA, PAIRS, 128).transpose(1, 0, 2)
    l2[:, 0:LORA, 1] = f["rwkv_a2"][0].reshape(LORA, PAIRS, 128).transpose(1, 0, 2)
    l2[:, :, 2:4] = f["rwkv_g2"][0].reshape(2, 128, PAIRS, 128).transpose(2, 1, 0, 3)
    rows = np.concatenate([f["meta_tokens"], f["x_prompt"][0], f["x_sample"].reshape(-1, D)], 0)
    vecs = [f["norm_mix"][0], f["norm_ffn"][0], f["norm_mix"][1], f["norm_ffn"][1], f["norm_out"], f["pool_scale"][0],
            *f["rwkv_mu"][0], f["rwkv_w0"][0], f["rwkv_a0"][0], f["rwkv_kk"][0], f["rwkv_ka"][0],
            f["rwkv_lnw"][0], f["rwkv_lnb"][0], f["rwkv_rk"][0].reshape(-1)]
    par = np.stack(vecs).reshape(len(vecs), KT, 128).transpose(2, 0, 1).reshape(128, NPAR)
    fp = np.concatenate([f["ffn_conv_w"], f["ffn_conv_b"][:, None]], 1)
    fp = fp.reshape(LAYERS, 4, 2 * FT, 128).transpose(0, 3, 2, 1)
    cst = f["state_ffn_conv"].reshape(LAYERS, NSEQ * 2, 2 * FT, 128).transpose(0, 3, 2, 1)
    s = f["state_rwkv_wkv"][0].reshape(NSEQ, PAIRS, 2, HS, HS)
    wkv = np.zeros((PAIRS, 2, HS, NSEQ, 2, HS), np.float32)
    for a in range(2):
        wkv[:, a, :, :, a, :] = s[:, :, a].transpose(1, 3, 0, 2)
    c = np.ascontiguousarray
    return {
        "W_all": units.reshape(4 * GROUPS, 128, 1024), "L2_all": l2.reshape(PAIRS, 128, 512), "xT": feat(rows),
        "params": c(par), "ffnpar": c(fp), "consts": constants(),
        "pool_st": feat(np.concatenate([f["state_pool"][0], np.zeros((NSEQ, TSAMPLE, D), np.float32)], 1)).reshape(128, KT, -1),
        "shift_st": feat(f["state_rwkv_shift"][0]), "wkv_st": wkv.reshape(PAIRS, 128, NSEQ * 128), "conv_st": c(cst),
    }


OUTPUTS = {"yT": (128, KT, TOK), "pool_out": (128, KT, PEXT - PROMPT), "shift_out": (128, KT, 9),
           "wkv_out": (PAIRS, 128, 9 * C), "conv_out": (LAYERS, 128, 2 * FT, 18)}
INPUTS = ["W_all", "L2_all", "xT", "params", "ffnpar", "consts", "pool_st", "shift_st", "wkv_st", "conv_st"]


def kernel(**inputs):
    import concourse.bacc as _bacc
    from concourse import mybir as _mybir
    from concourse.bass_utils import run_bass_kernel_spmd as _run

    arrays = lay_out(inputs)
    nc = _bacc.Bacc("TRN2", target_bir_lowering=False, num_devices=1)
    f32 = _mybir.dt.float32
    ins = [nc.dram_tensor(n, arrays[n].shape, f32, kind="ExternalInput").ap() for n in INPUTS]
    outs = [nc.dram_tensor(n, s, f32, kind="ExternalOutput").ap() for n, s in OUTPUTS.items()]
    spill = nc.dram_tensor("x_spill", (128, KT, TOK), f32, kind="Internal").ap()
    build(nc, *ins, *outs, spill)
    r = _run(nc, [arrays], core_ids=[0]).results[0]

    def rows(a):
        return np.ascontiguousarray(a.transpose(2, 1, 0).reshape(a.shape[2], D))

    y = rows(r["yT"])
    pool, shift = rows(r["pool_out"]), rows(r["shift_out"])
    w = r["wkv_out"].reshape(PAIRS, 2, HS, 9, HS).transpose(3, 0, 1, 4, 2).reshape(9, HEADS, HS, HS)
    cv = r["conv_out"].transpose(0, 3, 2, 1).reshape(LAYERS, 18, 2 * D_FF)
    c = np.ascontiguousarray
    return (c(y[N_META:PROMPT][None]), c(y[PROMPT:].reshape(NSEQ, TSAMPLE, D)),
            c(pool[None, None, 0:15]), c(pool[15:].reshape(1, NSEQ, 15 + TSAMPLE, D)[:, :, TSAMPLE:]),
            c(shift[None, 0:1]), c(shift[None, 1:9]),
            c(w[8][None, None]), c(w[0:8][None]),
            c(cv[:, None, 0:2]), c(cv[:, 2:18].reshape(LAYERS, NSEQ, 2, 2 * D_FF)))
```
